# Optimizing a Trainium2 kernel written in Bass

```python
import jax, jax.numpy as jnp
from jax import lax
import numpy as np

D_MODEL = 1024
BATCH = 1
SEQ = 256
DEPTH = 1

CHUNK = 64
Q_BLOCK = 128
SB_HEADS = 8
SB_HEAD_DIM = 64
SB_WIDTH = SB_HEADS * SB_HEAD_DIM
GLA_HEADS = 4
GLA_KEY_WIDTH = D_MODEL // 2
GLA_VALUE_WIDTH = D_MODEL
GLA_DK = GLA_KEY_WIDTH // GLA_HEADS
GLA_DV = GLA_VALUE_WIDTH // GLA_HEADS
GLA_GATE_RANK = 16
GLA_GATE_TAU = 16.0
D_FF = 4 * D_MODEL
EPS = 1e-6

SPLIT_SIZES = (SB_WIDTH, SB_WIDTH, SB_WIDTH,
               GLA_KEY_WIDTH, GLA_KEY_WIDTH, GLA_VALUE_WIDTH, GLA_VALUE_WIDTH, GLA_GATE_RANK,
               D_MODEL, D_MODEL)
D_IN = 3 * SB_WIDTH + 2 * GLA_KEY_WIDTH + 2 * GLA_VALUE_WIDTH + GLA_GATE_RANK + 2 * D_MODEL


def rms_norm(x, g):
    xf = x.astype(jnp.float32)
    y = xf * lax.rsqrt(jnp.mean(xf * xf, axis=-1, keepdims=True) + EPS)
    return (y * g.astype(jnp.float32)).astype(x.dtype)

def split_heads(t, n_heads):
    b, s, _ = t.shape
    return t.reshape(b, s, n_heads, -1).transpose(0, 2, 1, 3)

def merge_heads(t):
    b, h, s, d = t.shape
    return t.transpose(0, 2, 1, 3).reshape(b, s, h * d)

def stick_breaking_attention(q, k, v):
    _, _, s_len, d = q.shape
    scale = d ** -0.5
    outs = []
    for start in range(0, s_len, Q_BLOCK):
        end = start + Q_BLOCK
        kb = k[:, :, :end]
        vb = v[:, :, :end]
        z = jnp.einsum('bhtd,bhsd->bhts', q[:, :, start:end], kb) * scale
        t_idx = start + jnp.arange(Q_BLOCK)[:, None]
        s_idx = jnp.arange(end)[None, :]
        past = s_idx < t_idx
        log_beta = jax.nn.log_sigmoid(z)
        log_fail = jnp.where(past, log_beta - z, 0.0)
        later = lax.cumsum(log_fail, axis=3, reverse=True) - log_fail
        w = jnp.where(past, jnp.exp(log_beta + later), 0.0)
        outs.append(jnp.einsum('bhts,bhsd->bhtd', w, vb))
    return jnp.concatenate(outs, axis=2)

def gla_chunked(q, k, v, log_a):
    b, h, s_len, dk = q.shape
    dv = v.shape[-1]
    nc = s_len // CHUNK

    def to_chunks(t):
        return t.reshape(b, h, nc, CHUNK, t.shape[-1]).transpose(2, 0, 1, 3, 4)

    qc, kc, vc, ac = (to_chunks(t) for t in (q * dk ** -0.5, k, v, log_a))
    bc = jnp.cumsum(ac, axis=3)
    causal = jnp.tril(jnp.ones((CHUNK, CHUNK), dtype=bool))

    def step(state, inp):
        qi, ki, vi, bi = inp
        b_last = bi[:, :, -1:, :]
        o_inter = jnp.einsum('bhtk,bhkv->bhtv', qi * jnp.exp(bi), state)
        diff = bi[:, :, :, None, :] - bi[:, :, None, :, :]
        decay = jnp.exp(jnp.where(causal[:, :, None], diff, -jnp.inf))
        scores = jnp.einsum('bhtk,bhsk,bhtsk->bhts', qi, ki, decay)
        o_intra = jnp.einsum('bhts,bhsv->bhtv', scores, vi)
        new_state = (jnp.exp(b_last[:, :, 0, :, None]) * state
                     + jnp.einsum('bhsk,bhsv->bhkv', ki * jnp.exp(b_last - bi), vi))
        return new_state, o_inter + o_intra

    state0 = jnp.zeros((b, h, dk, dv), jnp.float32)
    _, o = lax.scan(step, state0, (qc, kc, vc, bc))
    return o.transpose(1, 2, 0, 3, 4).reshape(b, h, s_len, dv)

def first_inputs(seed: int = 0) -> dict:
    key = jax.random.key(seed)
    ks = jax.random.split(key, 16)
    f32 = jnp.float32

    def w(k, shape, fan_in):
        return jax.random.normal(k, shape, f32) * (fan_in ** -0.5)

    def gain(k, shape):
        return 1.0 + 0.02 * jax.random.normal(k, shape, f32)

    return {
        'x': jax.random.normal(ks[0], (BATCH, SEQ, D_MODEL), f32),
        'norm_mix': gain(ks[1], (DEPTH, D_MODEL)),
        'w_in': w(ks[2], (DEPTH, D_MODEL, D_IN), D_MODEL),
        'w_gate_up': w(ks[3], (DEPTH, GLA_GATE_RANK, GLA_KEY_WIDTH), GLA_GATE_RANK),
        'b_gate_up': 0.1 * jax.random.normal(ks[4], (DEPTH, GLA_KEY_WIDTH), f32),
        'gla_norm': gain(ks[5], (DEPTH, GLA_DV)),
        'w_proj_sb': w(ks[6], (DEPTH, SB_WIDTH, D_MODEL), SB_WIDTH),
        'w_proj_gla': w(ks[7], (DEPTH, GLA_VALUE_WIDTH, D_MODEL), GLA_VALUE_WIDTH),
        'w_out': w(ks[8], (DEPTH, D_MODEL, D_MODEL), D_MODEL),
        'norm_mlp': gain(ks[9], (DEPTH, D_MODEL)),
        'w_ff1': w(ks[10], (DEPTH, D_MODEL, D_FF), D_MODEL),
        'w_ff2': w(ks[11], (DEPTH, D_FF, D_MODEL), D_FF),
        'norm_final': gain(ks[12], (D_MODEL,)),
    }

def first_block(x, norm_mix, w_in, w_gate_up, b_gate_up, gla_norm, w_proj_sb, w_proj_gla,
              w_out, norm_mlp, w_ff1, w_ff2, norm_final):
    f32 = jnp.float32
    bsz, s_len, _ = x.shape
    split_points = np.cumsum(SPLIT_SIZES)[:-1].tolist()
    for layer in range(DEPTH):
        h = rms_norm(x, norm_mix[layer])
        proj = h @ w_in[layer]
        (sb_q, sb_k, sb_v, g_q, g_k, g_v, g_out, g_low, gate_sb, gate_gla) = jnp.split(
            proj, split_points, axis=-1)

        o_sb = stick_breaking_attention(split_heads(sb_q, SB_HEADS).astype(f32),
                                        split_heads(sb_k, SB_HEADS).astype(f32),
                                        split_heads(sb_v, SB_HEADS).astype(f32))
        o_sb = merge_heads(o_sb).astype(x.dtype)

        log_a = jax.nn.log_sigmoid((g_low @ w_gate_up[layer] + b_gate_up[layer]).astype(f32)) / GLA_GATE_TAU
        o_gla = gla_chunked(split_heads(g_q, GLA_HEADS).astype(f32),
                            split_heads(g_k, GLA_HEADS).astype(f32),
                            split_heads(g_v, GLA_HEADS).astype(f32),
                            split_heads(log_a, GLA_HEADS))
        o_gla = o_gla.transpose(0, 2, 1, 3)
        o_gla = rms_norm(o_gla, gla_norm[layer])
        o_gla = o_gla * jax.nn.silu(g_out.astype(f32).reshape(bsz, s_len, GLA_HEADS, GLA_DV))
        o_gla = o_gla.reshape(bsz, s_len, GLA_VALUE_WIDTH).astype(x.dtype)

        mix = (jax.nn.sigmoid(gate_sb) * (o_sb @ w_proj_sb[layer])
               + jax.nn.sigmoid(gate_gla) * (o_gla @ w_proj_gla[layer]))
        x = x + mix @ w_out[layer]

        h2 = rms_norm(x, norm_mlp[layer])
        x = x + jnp.square(jax.nn.relu(h2 @ w_ff1[layer])) @ w_ff2[layer]
    return rms_norm(x, norm_final)


MEM_LEN = 256
HEAD_DIM = 64
NSA_HEADS = 8
NSA_GROUPS = 2
NSA_HPG = NSA_HEADS // NSA_GROUPS
NSA_WIDTH = NSA_HEADS * HEAD_DIM
KV_WIDTH = NSA_GROUPS * HEAD_DIM
CMP_BLOCK = 32
CMP_STRIDE = 16
CMP_HIDDEN = 256
SLC_BLOCK = 64
SLC_TOPK = 16
WINDOW = 512
NSA_Q_BLOCK = 64
FORCE = 1e6
CONV_WIDTH = 512
CONV_KSIZE = 31
MEM_HEADS = 4
MEM_HEAD_DIM = 128
MEM_WIDTH = MEM_HEADS * MEM_HEAD_DIM
N_BRANCH = 3
D_FF_2 = -(-8 * D_MODEL // (3 * 256)) * 256
IN_COLS = NSA_WIDTH + 6 * KV_WIDTH + 3 * NSA_HEADS + 2 * CONV_WIDTH + MEM_WIDTH + N_BRANCH * D_MODEL
RMS_EPS = 1e-6
LN_EPS = 1e-5


def rms_norm_2(x, g):
    xf = x.astype(jnp.float32)
    y = xf * lax.rsqrt(jnp.mean(xf * xf, axis=-1, keepdims=True) + RMS_EPS)
    return (y * g.astype(jnp.float32)).astype(x.dtype)

def layer_norm(x, g, b):
    xf = x.astype(jnp.float32)
    mu = jnp.mean(xf, axis=-1, keepdims=True)
    var = jnp.mean(jnp.square(xf - mu), axis=-1, keepdims=True)
    y = (xf - mu) * lax.rsqrt(var + LN_EPS) * g.astype(jnp.float32) + b.astype(jnp.float32)
    return y.astype(x.dtype)

def masked_softmax(s, mask):
    s = jnp.where(mask, s.astype(jnp.float32), -jnp.inf)
    m = jnp.max(s, axis=-1, keepdims=True)
    m = jnp.where(jnp.isfinite(m), m, 0.0)
    e = jnp.exp(s - m)
    den = jnp.sum(e, axis=-1, keepdims=True)
    return e / jnp.where(den > 0, den, 1.0)

def compress_blocks(kv, pos, w1, w2):
    b, g, s, dh = kv.shape
    chunks = kv.reshape(b, g, s // CMP_STRIDE, CMP_STRIDE, dh)
    blocks = jnp.concatenate([chunks[:, :, :-1], chunks[:, :, 1:]], axis=3)
    blocks = (blocks + pos).reshape(b, g, blocks.shape[2], CMP_BLOCK * dh)
    return jax.nn.gelu(blocks @ w1) @ w2

def nsa_attention(q, kc, vc, ks, vs, kw, vw, gate):
    b, g, hpg, s, dh = q.shape
    n_c = kc.shape[2]
    n_sel = ks.shape[2]
    topk = min(SLC_TOPK, n_sel)
    ratio = SLC_BLOCK // CMP_STRIDE
    scale = dh ** -0.5
    qb_len = NSA_Q_BLOCK
    cmp_end = jnp.arange(n_c) * CMP_STRIDE + CMP_BLOCK - 1
    sel_ids = jnp.arange(n_sel)
    bi = jnp.arange(b)[:, None, None, None]
    gi = jnp.arange(g)[None, :, None, None]

    def block(qb):
        q0 = qb * qb_len
        t = q0 + jnp.arange(qb_len)
        qq = lax.dynamic_slice_in_dim(q, q0, qb_len, axis=3) * scale
        gg = lax.dynamic_slice_in_dim(gate, q0, qb_len, axis=3)

        s_c = jnp.einsum('bghqd,bgcd->bghqc', qq, kc)
        p_c = masked_softmax(s_c, cmp_end[None, :] <= t[:, None])
        o_c = jnp.einsum('bghqc,bgcd->bghqd', p_c.astype(vc.dtype), vc)

        imp = jnp.sum(p_c, axis=2)
        imp = jnp.pad(imp, ((0, 0), (0, 0), (0, 0), (1, ratio * (n_sel + 1) - n_c - 1)))
        rows = imp.reshape(b, g, qb_len, n_sel + 1, ratio)
        imp_s = jnp.sum(rows[..., :-1, :], axis=-1) + rows[..., 1:, 0]
        cur = t // SLC_BLOCK
        forced = (sel_ids[None, :] == 0) | (sel_ids[None, :] == cur[:, None]) | (sel_ids[None, :] == cur[:, None] - 1)
        future = sel_ids[None, :] * SLC_BLOCK > t[:, None]
        imp_s = jnp.where(forced, FORCE, jnp.where(future, -FORCE, imp_s))
        _, idx = lax.top_k(imp_s, topk)

        k_g = ks[bi, gi, idx]
        v_g = vs[bi, gi, idx]
        tok = idx[..., None] * SLC_BLOCK + jnp.arange(SLC_BLOCK)
        s_s = jnp.einsum('bghqd,bgqkld->bghqkl', qq, k_g).reshape(b, g, hpg, qb_len, topk * SLC_BLOCK)
        m_s = (tok <= t[:, None, None]).reshape(b, g, 1, qb_len, topk * SLC_BLOCK)
        p_s = masked_softmax(s_s, m_s).reshape(b, g, hpg, qb_len, topk, SLC_BLOCK)
        o_s = jnp.einsum('bghqkl,bgqkld->bghqd', p_s.astype(v_g.dtype), v_g)

        kwb = lax.dynamic_slice_in_dim(kw, q0, WINDOW + qb_len, axis=2)
        vwb = lax.dynamic_slice_in_dim(vw, q0, WINDOW + qb_len, axis=2)
        pos = q0 - WINDOW + jnp.arange(WINDOW + qb_len)
        diff = t[:, None] - pos[None, :]
        m_w = (diff >= 0) & (diff < WINDOW) & (pos[None, :] >= 0)
        s_w = jnp.einsum('bghqd,bgkd->bghqk', qq, kwb)
        p_w = masked_softmax(s_w, m_w)
        o_w = jnp.einsum('bghqk,bgkd->bghqd', p_w.astype(vwb.dtype), vwb)

        return gg[..., 0:1] * o_c + gg[..., 1:2] * o_s + gg[..., 2:3] * o_w

    out = lax.map(block, jnp.arange(s // qb_len))
    out = jnp.transpose(out, (1, 0, 4, 2, 3, 5))
    return out.reshape(b, s, g * hpg * dh)

def hybrid_layer(x, mem, norm_mix, w_in, nsa_qk_norm, cmp_pos, cmp_w1, cmp_w2, w_nsa_out,
                 conv_w, conv_b, conv_ln_g, conv_ln_b, w_conv_out, norm_mem, w_mem_kv,
                 mem_qk_norm, w_mem_out, w_out, norm_ffn, w_gate, w_up, w_down):
    b, s, _ = x.shape
    xn = rms_norm_2(x, norm_mix)
    proj = xn @ w_in
    sizes = [NSA_WIDTH, 6 * KV_WIDTH, 3 * NSA_HEADS, 2 * CONV_WIDTH, MEM_WIDTH, N_BRANCH * D_MODEL]
    points = [int(p) for p in np.cumsum(sizes)[:-1]]
    q_nsa, kv_nsa, g_nsa, conv_in, q_mem, g_merge = jnp.split(proj, points, axis=-1)

    def heads(t_, n):
        return jnp.transpose(t_.reshape(b, s, n, HEAD_DIM), (0, 2, 1, 3))
    q = rms_norm_2(heads(q_nsa, NSA_HEADS), nsa_qk_norm[0]).reshape(b, NSA_GROUPS, NSA_HPG, s, HEAD_DIM)
    k_c, v_c, k_s, v_s, k_w, v_w = [heads(t_, NSA_GROUPS) for t_ in jnp.split(kv_nsa, 6, axis=-1)]
    kc = rms_norm_2(compress_blocks(k_c, cmp_pos[0], cmp_w1[0], cmp_w2[0]), nsa_qk_norm[1])
    vc = compress_blocks(v_c, cmp_pos[1], cmp_w1[1], cmp_w2[1])
    n_sel = s // SLC_BLOCK
    ks = rms_norm_2(k_s, nsa_qk_norm[2]).reshape(b, NSA_GROUPS, n_sel, SLC_BLOCK, HEAD_DIM)
    vs = v_s.reshape(b, NSA_GROUPS, n_sel, SLC_BLOCK, HEAD_DIM)
    pad = ((0, 0), (0, 0), (WINDOW, 0), (0, 0))
    kw = jnp.pad(rms_norm_2(k_w, nsa_qk_norm[3]), pad)
    vw = jnp.pad(v_w, pad)
    gate = jnp.transpose(jax.nn.sigmoid(g_nsa).reshape(b, s, NSA_GROUPS, NSA_HPG, 3), (0, 2, 3, 1, 4))
    o_nsa = nsa_attention(q, kc, vc, ks, vs, kw, vw, gate)
    br_nsa = o_nsa @ w_nsa_out

    a, ag = jnp.split(conv_in, 2, axis=-1)
    u = a * jax.nn.sigmoid(ag)
    u = jnp.pad(u, ((0, 0), (CONV_KSIZE - 1, 0), (0, 0)))
    u = lax.conv_general_dilated(u, conv_w, (1,), 'VALID', dimension_numbers=('NWC', 'WIO', 'NWC'),
                                 feature_group_count=CONV_WIDTH) + conv_b
    u = jax.nn.silu(layer_norm(u, conv_ln_g, conv_ln_b))
    br_conv = u @ w_conv_out

    qm = rms_norm_2(q_mem.reshape(b, s, MEM_HEADS, MEM_HEAD_DIM), mem_qk_norm[0])
    kvm = rms_norm_2(mem, norm_mem) @ w_mem_kv
    km, vm = jnp.split(kvm, 2, axis=-1)
    km = rms_norm_2(km.reshape(b, -1, MEM_HEADS, MEM_HEAD_DIM), mem_qk_norm[1])
    vm = vm.reshape(b, -1, MEM_HEADS, MEM_HEAD_DIM)
    s_m = jnp.einsum('bshd,bmhd->bhsm', qm, km).astype(jnp.float32) * (MEM_HEAD_DIM ** -0.5)
    p_m = jax.nn.softmax(s_m, axis=-1)
    o_m = jnp.einsum('bhsm,bmhd->bshd', p_m.astype(vm.dtype), vm).reshape(b, s, MEM_WIDTH)
    br_mem = o_m @ w_mem_out

    gm = jax.nn.sigmoid(g_merge).reshape(b, s, N_BRANCH, D_MODEL)
    merged = gm[:, :, 0] * br_nsa + gm[:, :, 1] * br_conv + gm[:, :, 2] * br_mem
    h = x + merged @ w_out

    hn = rms_norm_2(h, norm_ffn)
    return h + (jax.nn.silu(hn @ w_gate) * (hn @ w_up)) @ w_down

def second_inputs(seed: int = 0) -> dict:
    key = jax.random.key(seed)
    k = jax.random.split(key, 24)
    f32 = jnp.float32
    L = DEPTH

    def nrm(kk, shape, fan_in):
        return jax.random.normal(kk, shape, f32) * (fan_in ** -0.5)

    def gain(kk, shape):
        return 1.0 + 0.02 * jax.random.normal(kk, shape, f32)

    def small(kk, shape):
        return 0.01 * jax.random.normal(kk, shape, f32)

    return {
        "x": jax.random.normal(k[0], (BATCH, SEQ, D_MODEL), f32),
        "mem": jax.random.normal(k[1], (BATCH, MEM_LEN, D_MODEL), f32),
        "norm_mix": gain(k[2], (L, D_MODEL)),
        "w_in": nrm(k[3], (L, D_MODEL, IN_COLS), D_MODEL),
        "nsa_qk_norm": gain(k[4], (L, 4, HEAD_DIM)),
        "cmp_pos": 2.0 * small(k[5], (L, 2, CMP_BLOCK, HEAD_DIM)),
        "cmp_w1": nrm(k[6], (L, 2, CMP_BLOCK * HEAD_DIM, CMP_HIDDEN), CMP_BLOCK * HEAD_DIM),
        "cmp_w2": nrm(k[7], (L, 2, CMP_HIDDEN, HEAD_DIM), CMP_HIDDEN),
        "w_nsa_out": nrm(k[8], (L, NSA_WIDTH, D_MODEL), NSA_WIDTH),
        "conv_w": nrm(k[9], (L, CONV_KSIZE, 1, CONV_WIDTH), CONV_KSIZE),
        "conv_b": small(k[10], (L, CONV_WIDTH)),
        "conv_ln_g": gain(k[11], (L, CONV_WIDTH)),
        "conv_ln_b": small(k[12], (L, CONV_WIDTH)),
        "w_conv_out": nrm(k[13], (L, CONV_WIDTH, D_MODEL), CONV_WIDTH),
        "norm_mem": gain(k[14], (L, D_MODEL)),
        "w_mem_kv": nrm(k[15], (L, D_MODEL, 2 * MEM_WIDTH), D_MODEL),
        "mem_qk_norm": gain(k[16], (L, 2, MEM_HEAD_DIM)),
        "w_mem_out": nrm(k[17], (L, MEM_WIDTH, D_MODEL), MEM_WIDTH),
        "w_out": nrm(k[18], (L, D_MODEL, D_MODEL), D_MODEL),
        "norm_ffn": gain(k[19], (L, D_MODEL)),
        "w_gate": nrm(k[20], (L, D_MODEL, D_FF_2), D_MODEL),
        "w_up": nrm(k[21], (L, D_MODEL, D_FF_2), D_MODEL),
        "w_down": nrm(k[22], (L, D_FF_2, D_MODEL), D_FF_2),
    }

def second_block(x, mem, norm_mix, w_in, nsa_qk_norm, cmp_pos, cmp_w1, cmp_w2, w_nsa_out,
              conv_w, conv_b, conv_ln_g, conv_ln_b, w_conv_out, norm_mem, w_mem_kv,
              mem_qk_norm, w_mem_out, w_out, norm_ffn, w_gate, w_up, w_down):
    h = x
    for l in range(DEPTH):
        h = hybrid_layer(h, mem, norm_mix[l], w_in[l], nsa_qk_norm[l], cmp_pos[l], cmp_w1[l], cmp_w2[l],
                         w_nsa_out[l], conv_w[l], conv_b[l], conv_ln_g[l], conv_ln_b[l], w_conv_out[l],
                         norm_mem[l], w_mem_kv[l], mem_qk_norm[l], w_mem_out[l], w_out[l], norm_ffn[l],
                         w_gate[l], w_up[l], w_down[l])
    return h


def setup_inputs(seed=0):
    out = dict(first_inputs(seed))
    for name, value in second_inputs(seed + 1).items():
        if name != "x":
            out[name + "_2"] = value
    return out


def reference(
    x, norm_mix, w_in, w_gate_up, b_gate_up, gla_norm, w_proj_sb, w_proj_gla, w_out, norm_mlp,
    w_ff1, w_ff2, norm_final, mem_2, norm_mix_2, w_in_2, nsa_qk_norm_2, cmp_pos_2, cmp_w1_2,
    cmp_w2_2, w_nsa_out_2, conv_w_2, conv_b_2, conv_ln_g_2, conv_ln_b_2, w_conv_out_2,
    norm_mem_2, w_mem_kv_2, mem_qk_norm_2, w_mem_out_2, w_out_2, norm_ffn_2, w_gate_2, w_up_2,
    w_down_2,
):
    x = first_block(
        x, norm_mix, w_in, w_gate_up, b_gate_up, gla_norm, w_proj_sb, w_proj_gla, w_out,
        norm_mlp, w_ff1, w_ff2, norm_final,
    )
    return second_block(
        x, mem_2, norm_mix_2, w_in_2, nsa_qk_norm_2, cmp_pos_2, cmp_w1_2, cmp_w2_2, w_nsa_out_2,
        conv_w_2, conv_b_2, conv_ln_g_2, conv_ln_b_2, w_conv_out_2, norm_mem_2, w_mem_kv_2,
        mem_qk_norm_2, w_mem_out_2, w_out_2, norm_ffn_2, w_gate_2, w_up_2, w_down_2,
    )


_drawn_inputs = setup_inputs


def setup_inputs(seed=0):
    import zlib

    import numpy as np

    out = dict(_drawn_inputs(seed))
    spreads = {}
    factors = {'norm_mix': 2.883,
     'b_gate_up': 3.609,
     'gla_norm': 7.306,
     'norm_mlp': 2.903,
     'norm_mix_2': 5.996,
     'nsa_qk_norm_2': 8.0,
     'cmp_pos_2': 51.432,
     'conv_b_2': 34.379,
     'conv_ln_g_2': 97.768,
     'conv_ln_b_2': 181.575,
     'norm_mem_2': 8.0,
     'mem_qk_norm_2': 8.0,
     'norm_ffn_2': 14.34}
    for name, (base, spread) in spreads.items():
        noise = np.random.default_rng([zlib.crc32(name.encode()), seed]).standard_normal(out[name].shape)
        drawn = base * np.exp(spread * noise) if base else spread * noise
        out[name] = __import__('jax').numpy.asarray(drawn.astype(out[name].dtype))
    for name, factor in factors.items():
        out[name] = (out[name] * factor).astype(out[name].dtype)
    return out
```

```python
from contextlib import ExitStack

import numpy as np

import concourse.bass as bass
from concourse import mybir

F32 = mybir.dt.float32
F32R = mybir.dt.float32r
ALU = mybir.AluOpType
ACT = mybir.ActivationFunctionType
AX = mybir.AxisListType.X

P = 128
D = 1024
T = 256
KT = D // P
TT = T // P
CW = 256
EPS = 1e-6
SB_H, SB_D = 8, 64
GLA_H, GLA_DK, GLA_DV = 4, 128, 256
RANK = 16
LEVELS = 7
D_FF = 4096
D_FF2 = 2816
SHARE = 1536
RING = 3


def two_block_kernel(
    nc, x, norm_mix, w_in, w_gate_up, b_gate_up, gla_norm, w_proj_sb, w_proj_gla, w_out, norm_mlp,
    w_ff1, w_ff2, norm_final, mem_2, norm_mix_2, w_in_2, nsa_qk_norm_2, cmp_pos_2, cmp_w1_2,
    cmp_w2_2, w_nsa_out_2, conv_w_2, conv_b_2, conv_ln_g_2, conv_ln_b_2, w_conv_out_2, norm_mem_2,
    w_mem_kv_2, mem_qk_norm_2, w_mem_out_2, w_out_2, norm_ffn_2, w_gate_2, w_up_2, w_down_2, out,
):
    def cols(w, c0, width=CW):
        return w[0].rearrange("(k p) n -> p k n", p=P)[:, :, c0:c0 + width]

    def rows(w, r0):
        return w[0].rearrange("(k p) n -> p k n", p=P)[:, r0:r0 + 2, :]

    chunks, at = [], {}

    def chunk(name, src):
        at[name] = len(chunks)
        chunks.append(src)

    sbq0, sbk0, sbv0, gq0, gk0, gv0, go0, low0, gs0, gg0 = np.cumsum(
        [0, 512, 512, 512, 512, 512, 1024, 1024, 16, 1024]).tolist()
    chunk("low", cols(w_in, low0, P))
    for name, c0, count in (("sbq", sbq0, 2), ("sbk", sbk0, 2), ("gq", gq0, 2), ("gk", gk0, 2), ("sbv", sbv0, 2),
                            ("gv", gv0, 4), ("gates", gs0, 4), ("gateg", gg0, 4)):
        for c in range(count):
            chunk(f"{name}{c}", cols(w_in, c0 + c * CW))
            if name == "gv":
                chunk(f"gout{c}", cols(w_in, go0 + c * CW))
    for c in range(2):
        chunk(f"projs{c}", cols(w_proj_sb, 512 * c, 512))
    for c in range(4):
        chunk(f"projg{c}", cols(w_proj_gla, CW * c))
    for c in range(4):
        chunk(f"wout{c}", rows(w_out, 2 * c))
    for c in range(2):
        chunk(f"km{c}", cols(w_mem_kv_2, CW * c))
    F1 = D_FF // CW
    FFN1 = len(chunks)
    ff1_src = w_ff1[0].rearrange("(k p) (c n) -> c p k n", p=P, n=CW)
    ff2_src = w_ff2[0].rearrange("(c k p) n -> c p k n", p=P, k=2)
    after_ffn1 = FFN1 + 2 * F1
    chunks += [None] * (2 * F1)
    for c in range(2):
        chunk(f"vm{c}", cols(w_mem_kv_2, 512 + CW * c))
    ca0, cg0, qm0, g20, g10, g00 = 1304, 1816, 2328, 4888, 3864, 2840
    for c in range(2):
        chunk(f"ca{c}", cols(w_in_2, ca0 + CW * c))
        chunk(f"cg{c}", cols(w_in_2, cg0 + CW * c))
    def compress_chunk(b, c):
        chunk(f"w{'kv'[b]}{c}", cmp_w1_2[0, b].rearrange("(m p) n -> p m n", p=P)[:, 8 * c:8 * c + 8, :])

    chunk("kcvc", cols(w_in_2, 512))
    for c in range(2):
        chunk(f"qm{c}", cols(w_in_2, qm0 + CW * c))
    for c, name in enumerate(("ksvs", "kwvw")):
        chunk(name, cols(w_in_2, 768 + CW * c))
        compress_chunk(0, c)
    for c in range(2):
        chunk(f"q{c}", cols(w_in_2, CW * c))
        compress_chunk(1, c)
    for name, c0, w in (("gm", g20, w_mem_out_2), ("gc", g10, w_conv_out_2), ("gn", g00, w_nsa_out_2)):
        for c in range(4):
            chunk(f"{name}{c}", cols(w_in_2, c0 + CW * c))
        for c in range(2):
            chunk(f"o{name}{c}", cols(w, 512 * c, 512))
    for c in range(4):
        chunk(f"xout{c}", rows(w_out_2, 2 * c))
    F2 = D_FF2 // CW
    FFN2 = len(chunks)
    gate_src, up_src = (w[0].rearrange("(k p) (c n) -> c p k n", p=P, n=CW) for w in (w_gate_2, w_up_2))
    down_src = w_down_2[0].rearrange("(c k p) n -> c p k n", p=P, k=2)
    ATT = [("m", a, 0) for a in range(TT)] + [(k, a, g) for a in range(TT) for g in range(2) for k in "swc"]

    with ExitStack() as ctx:
        def sb(name, shape, dt=F32):
            return ctx.enter_context(nc.sbuf_tensor(name, shape, dt))

        def sem(name):
            return ctx.enter_context(nc.semaphore(name))

        PRMS = 13
        SIG = [name for name in at if name[:4] in ("gout", "gate") or name[:2] in ("cg", "gm", "gc", "gn")]
        SIG_EXP = [f"gout{c}" for c in range(4)] + ["cg0", "cg1"]
        FN_WAIT = [["km0"], ["km1"], ["qm0"], ["qm1"], [], [], ["q0"], ["q1"], []]
        CONSTS = 1 + 1 + 4 * LEVELS + 1 + 3 + 1 + 3 * LEVELS + 1
        PS = ctx.enter_context(nc.psum_tensor("PS", [P, 8, 512], F32))
        raw = sb("raw", [P, RING, 2048])
        whi = sb("whi", [P, RING, 2048], F32R)
        wlo = sb("wlo", [P, RING, 2048], F32R)
        res = sb("res", [P, TT, D])
        xn = sb("xn", [P, TT, D])
        hT_hi = sb("hT_hi", [P, KT, T], F32R)
        hT_lo = sb("hT_lo", [P, KT, T], F32R)
        oT_hi = sb("oT_hi", [P, 12, T], F32R)
        oT_lo = sb("oT_lo", [P, 12, T], F32R)
        aT_hi = sb("aT_hi", [P, RING, 2, T], F32R)
        aT_lo = sb("aT_lo", [P, RING, 2, T], F32R)
        AR = sb("AR", [P, 9216])
        TMP = sb("TMP", [P, 4736])
        relu = sb("relu", [P, RING, 512])
        ident = sb("ident", [P, P])
        negtri = sb("negtri", [P, P])
        negone = sb("negone", [P, P])
        prm = sb("prm", [P, 92])
        cw = sb("cw", [P, 4, 31])
        wgn = sb("wgn", [P, KT, 24])
        w2k = sb("w2k", [P, 2, 2, 64])
        w2v = sb("w2v", [P, 2, 64])
        stat = sb("stat", [P, 6, 8])
        gstat = sb("gstat", [P, GLA_H, 8])
        eps = sb("eps", [P, 1])
        mhalf = sb("mhalf", [P, 6])
        conv_product = sb("conv_product", [P, 2, T])

        qT_sb = AR[:, 0:1024].rearrange("p (f t) -> p f t", f=4)
        kT_sb = AR[:, 1024:2048].rearrange("p (f t) -> p f t", f=4)
        v_sb = AR[:, 2048:3072].rearrange("p (a n) -> p a n", a=TT)
        gqT = AR[:, 3072:4096].rearrange("p (f t) -> p f t", f=4)
        gkT = AR[:, 4096:5120].rearrange("p (f t) -> p f t", f=4)
        gv = AR[:, 5120:7168].rearrange("p (a n) -> p a n", a=TT)
        gsil = AR[:, 7168:9216].rearrange("p (a n) -> p a n", a=TT)
        gate_s = AR[:, 0:2048].rearrange("p (f t) -> p f t", f=KT)
        gate_g = xn[:, :, :].rearrange("p a (f t) -> p (a f) t", t=T)
        a_ls = xn[:, 0, :].rearrange("p (a n) -> p a n", a=TT)
        sb_w = xn[:, 1, 0:768].rearrange("p (b n) -> p b n", b=2)
        junk_g = xn[:, 1, 768:1024]
        memx = gv
        glow = AR[0:RANK, 7168:7424]
        wup = AR[0:RANK, 7424:7936]
        bup = AR[0:1, 7936:8448]
        onerow = AR[0:1, 8448:8576]
        prm_rows = AR[0:92, 8576:8704]
        sbt = res[:, :, 0:768].rearrange("p b (i n) -> p b i n", i=2)
        decay_sum = TMP[:, 0:1152].rearrange("p (l t) -> p l t", t=P)
        mask = TMP[:, 1152:2176].rearrange("p (l t) -> p l t", t=P)
        E = TMP[:, 2176:3200].rearrange("p (l t) -> p l t", t=P)
        QK = TMP[:, 3200:4096].rearrange("p (l t) -> p l t", t=P)
        sq = TMP[:, 3200:4736].rearrange("p (j n) -> p j n", j=RING)
        kmT = AR[:, 0:1024].rearrange("p (f t) -> p f t", f=4)
        K7 = TMP[:, 4096:4224]
        Q7 = TMP[:, 4224:4352]
        gfin = E.rearrange("p l t -> p (l t)")
        ACC_FLAT = [PS[:, 2 * a:2 * a + 2, :].rearrange("p b n -> p (b n)") for a in range(TT)]
        S_gla = TMP[:, 4352:4736].rearrange("p (i t) -> p i t", t=P)

        G = AR[:, 0:2048].rearrange("p (f t) -> p f t", f=KT)
        vm = AR[:, 1024:2048].rearrange("p (a n) -> p a n", a=TT)
        qm = AR[:, 2048:3072].rearrange("p (f t) -> p f t", f=4)
        qn = AR[:, 3072:4096].rearrange("p (f t) -> p f t", f=4)
        kdup = {"s": AR[:, 4096:4608].rearrange("p (g t) -> p g t", g=2),
                "w": AR[:, 4608:5120].rearrange("p (g t) -> p g t", g=2)}
        vn = {"s": AR[:, 5120:5376].rearrange("p (a n) -> p a n", a=TT),
              "w": AR[:, 5376:5632].rearrange("p (a n) -> p a n", a=TT)}
        PAD = 30
        u_conv = AR[:, 5632:6776].rearrange("p (f t) -> p f t", f=4)
        u_flat = AR[:, 5632:6656]
        cacc = AR[:, 6776:7800].rearrange("p (f t) -> p f t", f=4)
        cacc_flat = AR[:, 6776:7800]
        cw_rows = AR[0:31, 6776:7288]
        Z = [AR[:, 7800 + 512 * b:8312 + 512 * b].rearrange("p (g t) -> p g t", g=2) for b in range(2)]
        kcT = AR[:, 8824:8854]
        vc = AR[0:15, 8854:8982].rearrange("p (g n) -> p g n", g=2)
        hid = [AR[:, 8982 + 60 * b:9042 + 60 * b] for b in range(2)]
        gn24 = AR[:, 9102:9150]
        hwork = AR[:, 9150:9210]
        Mg = xn[:, :, :].rearrange("p a (f t) -> p (a f) t", t=T)
        fsq, fvar = xn[:, 0, 0:512], xn[:, 0, 512:1024]
        fy = relu[:, 2, :]
        blk = [xn[:, 1, 512 * b:512 * b + 480].rearrange("p (m i) -> p m i", m=16) for b in range(2)]
        blk_hi, blk_lo = ([w[:, b].rearrange("p a t -> p (a t)")[:, 0:480].rearrange("p (m i) -> p m i", m=16)
                           for b in range(2)] for w in (aT_hi, aT_lo))
        pbuf = TMP[:, 0:2048].rearrange("p (b n) -> p b n", b=2)
        pT = TMP[:, 2048:4096].rearrange("p (b n) -> p b n", b=2)
        causal = TMP[:, 4096:4352]
        cmask = TMP[:, 4352:4382].rearrange("p (a i) -> p a i", a=TT)
        amax = TMP[:, 4382:4438].rearrange("p (u h) -> p u h", h=4)
        aden = TMP[:, 4438:4494].rearrange("p (u h) -> p u h", h=4)
        acoef = TMP[:, 4494:4550].rearrange("p (u h) -> p u h", h=4)

        x_in, prm_in, gfin_in, gup_in, mem_in, x_again = (
            sem(n) for n in ("x_in", "prm_in", "gfin_in", "gup_in", "mem_in", "x_again"))
        landed = [sem(f"landed{i}") for i in range(RING)]
        hi_made, lo_made, lob_made, chunk_used = sem("hi_made"), sem("lo_made"), sem("lob_made"), sem("chunk_used")
        drained = [sem("drained0"), sem("drained1")]
        const_made, ident_made = sem("const_made"), sem("ident_made")
        prm_tr, prm_made = sem("prm_tr"), sem("prm_made")
        ssq_made, var_made, ln_made, exp_made, newton, rs_made, xn_made = (
            sem(n) for n in ("ssq_made", "var_made", "ln_made", "exp_made", "newton", "rs_made", "xn_made"))
        tr_made, trhi_made, trlo_made = sem("tr_made"), sem("trhi_made"), sem("trlo_made")
        evac_exp, evac_dve = sem("evac_exp"), sem("evac_dve")
        sb_z, sb_abs, sb_e, sb_l, sb_sp, sb_spm, sb_rc, sb_wm, sb_wk, sb_pv, sb_hi, sb_lo = (
            sem(n) for n in ("sb_z", "sb_abs", "sb_e", "sb_l", "sb_sp", "sb_spm", "sb_rc", "sb_wm", "sb_wk", "sb_pv", "sb_hi", "sb_lo"))
        ga_low, ga_y, ga_abs, ga_e, ga_l, ga_made = (sem(n) for n in ("ga_low", "ga_y", "ga_abs", "ga_e", "ga_l", "ga_made"))
        gf_sum, gf_exp, gf_qk, gs_made, gs_masked, gs_ready, gs_x = (
            sem(n) for n in ("gf_sum", "gf_exp", "gf_qk", "gs_made", "gs_masked", "gs_ready", "gs_x"))
        go_made, go_ssq, go_var, go_ln, go_exp, go_newt, go_rs, go_norm, go_tr, go_hi, go_lo = (
            sem(n) for n in ("go_made", "go_ssq", "go_var", "go_ln", "go_exp", "go_newt", "go_rs", "go_norm", "go_tr", "go_hi", "go_lo"))
        mix_a, mix_b, mix_hi, mix_lo = sem("mix_a"), sem("mix_b"), sem("mix_hi"), sem("mix_lo")
        h1_relu, h1_sq, h1_hi, h1_lo = (sem(n) for n in ("h1_relu", "h1_sq", "h1_hi", "h1_lo"))
        dve_link = sem("dve_link")
        att_s, att_m, att_max, att_e, att_den, att_coef, att_p, att_t, att_pt, att_o, att_oc, att_hi, att_lo = (
            sem(n) for n in ("att_s", "att_m", "att_max", "att_e", "att_den", "att_coef", "att_p", "att_t", "att_pt", "att_o", "att_oc", "att_hi", "att_lo"))
        fn_sq, fn_sum, fn_var, fn_ln, fn_exp, fn_made, kd_made = (
            sem(n) for n in ("fn_sq", "fn_sum", "fn_var", "fn_ln", "fn_exp", "fn_made", "kd_made"))
        cw_in, cw_tr, cw_made, pad_made, mask2_made, small2_in = (
            sem(n) for n in ("cw_in", "cw_tr", "cw_made", "pad_made", "mask2_made", "small2_in"))
        gn_clip, mhalf_made = sem("gn_clip"), sem("mhalf_made")
        gn_sum, gn_exp, gn_made = sem("gn_sum"), sem("gn_exp"), sem("gn_made")
        sg_ln, sg_min, sg_exp = sem("sg_ln"), sem("sg_min"), sem("sg_exp")
        raw_made, z_made, blk_made, blk_hid, blk_lod = (sem(n) for n in ("raw_made", "z_made", "blk_made", "blk_hid", "blk_lod"))
        h_raw, h_arg, h_exp, h_made, kc_sum, vc_made, kc_raw = (
            sem(n) for n in ("h_raw", "h_arg", "h_exp", "h_made", "kc_sum", "vc_made", "kc_raw"))
        taps_b = sem("taps_b")
        taps, cv_mean, cv_mid, cv_sq, cv_var, cv_v, cv_ln, cv_exp, cv_y, cv_lin, cv_abs, cv_l, cv_m, cv_sig, cv_f, cv_hi, cv_lo = (
            sem(n) for n in ("taps", "cv_mean", "cv_mid", "cv_sq", "cv_var", "cv_v", "cv_ln", "cv_exp", "cv_y", "cv_lin",
                             "cv_abs", "cv_l", "cv_m", "cv_sig", "cv_f", "cv_hi", "cv_lo"))
        merged, mhi_made, mlo_made = sem("merged"), sem("mhi_made"), sem("mlo_made")
        act_link = sem("act_link")
        s_e = sem("s_e")
        s_abs, s_ln, s_min, s_sig, s_mul, s_prod, s_hi, s_lo = (
            sem(n) for n in ("s_abs", "s_ln", "s_min", "s_sig", "s_mul", "s_prod", "s_hi", "s_lo"))
        out_a, out_b = sem("out_a"), sem("out_b")
        x3_made, out_done = sem("x3_made"), sem("out_done")

        ACC = [PS[:, 2 * a:2 * a + 2, :] for a in range(TT)]

        unit_of, units = {}, 0
        for name in at:
            if name in ("wk1", "wv1"):
                unit_of[name] = unit_of[name[:2] + "0"]
            elif not name.startswith(("wout", "xout")):
                unit_of[name] = units
                units += 2 if name.startswith(("projs", "o")) else 1

        units_before_ffn1 = unit_of["vm0"]

        def lin(u):
            return PS[:, 4 + u % 2, :]

        def seq(w, s):
            return w[:, s, :]

        G_MIX, G_MLP, G_MIX2, G_MEM, G_FFN, G_GLA, B_CONV, LN_G, LN_B, G_MQK, G_NSA, POS = (
            0, 8, 16, 24, 32, 40, 42, 46, 50, 54, 56, 60)

        FN = [(kmT[:, 0:2, :], 512, P, G_MQK + 1), (kmT[:, 2:4, :], 512, P, G_MQK + 1),
              (qm[:, 0:2, :], 512, P, G_MQK), (qm[:, 2:4, :], 512, P, G_MQK),
              (kdup["s"][:, 0, :], T, 64, G_NSA + 2), (kdup["w"][:, 0, :], T, 64, G_NSA + 3),
              (qn[:, 0:2, :], 512, 64, G_NSA), (qn[:, 2:4, :], 512, 64, G_NSA),
              (kcT, 30, 64, G_NSA + 1)]
        FN_AT = [1, 2, 6, 7, 8, 10, 12, 14, 16]

        def scratch(e):
            width = FN[e][1]
            if e == 8:
                return hwork[:, 0:30], hwork[:, 30:60], fy[:, 0:30]
            w = fsq if e % 2 == 0 else AR[:, 3072:3584] if e < 7 else AR[:, 0:512]
            return w[:, 0:width], fvar[:, 0:width], fy[:, 0:width]

        def key_tiles(i):
            kind, a, g = ATT[i]
            return 2 if kind == "m" else 1 if kind == "c" else a + 1

        def group_of(i):
            return i if i < 2 else 2 + (i - 2) // 3

        POOL_LO = range(at["ca0"] + 2, FFN2)

        block = ctx.enter_context(nc.Block())

        @block.sync
        def _(sp):
            sp.dma_start(res[:, :, :], x[0].rearrange("(a p) n -> p a n", p=P)).then_inc(x_in, 16)

            def load(n, src, it=0):
                if n >= RING:
                    sp.wait_ge(lo_made, n - RING + 1 + 6 * it)
                if n - RING in POOL_LO:
                    sp.wait_ge(lob_made, n - RING - POOL_LO[0] + 1)
                width = src.shape[1] * src.shape[2]
                sp.dma_start(raw[:, n % RING, 0:width].rearrange("p (k n) -> p k n", n=src.shape[2]),
                             src).then_inc(landed[n % RING], 16)

            for n in range(FFN1):
                load(n, chunks[n])
            load(FFN1, ff1_src[0])
            with sp.Fori(0, (F1 - 1) // 3) as it:
                for j in range(3):
                    load(FFN1 + 1 + 2 * j, ff1_src[3 * it + j + 1], it)
                    load(FFN1 + 2 + 2 * j, ff2_src[3 * it + j], it)
            load(after_ffn1 - 1, ff2_src[F1 - 1])
            for n in range(after_ffn1, FFN2):
                load(n, chunks[n])
            load(FFN2, gate_src[0])
            load(FFN2 + 1, up_src[0])
            with sp.Fori(0, 5) as it:
                for j in range(2):
                    load(FFN2 + 2 + 3 * j, gate_src[2 * it + j + 1], it)
                    load(FFN2 + 3 + 3 * j, up_src[2 * it + j + 1], it)
                    load(FFN2 + 4 + 3 * j, down_src[2 * it + j], it)
            load(FFN2 + 32, down_src[F2 - 1])
            out_v = out[0].rearrange("(a p) n -> a p n", p=P)
            sp.wait_ge(out_a, 1)
            sp.dma_start(out_v[0], res[:, 0, :]).then_inc(out_done, 16)
            sp.wait_ge(out_b, 1)
            sp.dma_start(out_v[1], res[:, 1, :]).then_inc(out_done, 16)
            sp.wait_ge(out_done, 32)

        @block.gpsimd
        def _(pool):
            made = [0]

            def step(ins):
                made[0] += 1
                ins.then_inc(const_made, 1)
                pool.wait_ge(const_made, made[0])

            def keep(view, pattern, base, mult, op=ALU.is_ge, fill=0.0):
                step(pool.affine_select(out=view, in_=view, compare_op=op, fill=fill, base=base,
                                        pattern=pattern, channel_multiplier=mult))

            pool.memset(ident[:, :], 0.0).then_inc(ident_made, 1)
            pool.wait_ge(ident_made, 1)
            pool.affine_select(out=ident[:, :], in_=ident[:, :], compare_op=ALU.not_equal, fill=1.0, base=0,
                               pattern=[[-1, P]], channel_multiplier=1).then_inc(ident_made, 1)
            pool.memset(onerow, 1.0).then_inc(ident_made, 1)
            pool.memset(eps[:, :], EPS).then_inc(ident_made, 1)
            step(pool.memset(decay_sum, 1.0))
            keep(decay_sum[:, 0, :], [[-1, P]], 0, 1, ALU.is_gt)
            for l in range(LEVELS):
                h = 1 << l
                v = decay_sum[:, 1 + l, :].rearrange("p (b s x) -> p b s x", s=2, x=h)
                nb = P // (2 * h)
                keep(v[:, :, 1, :], [[-2 * h, nb], [0, h]], -h, 1)
                keep(v[:, :, 1, :], [[2 * h, nb], [1, h]], h, -1)
                keep(v[:, :, 0, :], [[-2 * h, nb], [-1, h]], 0, 1, ALU.is_gt)
                keep(v[:, :, 0, :], [[2 * h, nb], [0, h]], h, -1, ALU.is_gt)
            keep(decay_sum[:, 8, :], [[1, P]], 0, -1)
            step(pool.memset(negone[:, :], -1.0))
            step(pool.memset(negtri[:, :], -1.0))
            keep(negtri[:, :], [[-1, P]], 0, 1)
            step(pool.memset(mask, 0.0))
            for l in range(LEVELS):
                h = 1 << l
                v = mask[:, l, :].rearrange("p (b s x) -> p b s x", s=2, x=h)[:, :, 1, :]
                nb = P // (2 * h)
                step(pool.memset(v, 1.0))
                keep(v, [[-2 * h, nb], [0, h]], 0, 1)
                keep(v, [[2 * h, nb], [0, h]], h, -1, ALU.is_gt)
            keep(mask[:, LEVELS, :], [[-1, P]], 0, 1, ALU.not_equal, 1.0)

            def sb_mask_sp(h):
                v = sbt[:, h % 2, 1, :].rearrange("p (i t) -> p i t", t=P)[:, 0:3:2, :]
                pool.wait_ge(sb_sp, h + 1)
                pool.affine_select(out=v, in_=v, compare_op=ALU.is_gt, fill=0.0, base=0,
                                   pattern=[[0, 2], [1, P]], channel_multiplier=-1).then_inc(sb_spm, 1)

            def sb_mask_w(h):
                v = sb_w[:, h % 2, :].rearrange("p (i t) -> p i t", t=P)[:, 0:3:2, :]
                pool.wait_ge(sb_wm, h + 1)
                pool.affine_select(out=v, in_=v, compare_op=ALU.is_gt, fill=0.0, base=0,
                                   pattern=[[0, 2], [1, P]], channel_multiplier=-1).then_inc(sb_wk, 1)

            def gla_factors(u):
                h, a = u // 2, u % 2
                pool.wait_ge(gf_exp, u + 1)
                pool.wait_ge(drained[unit_of["gk1"] % 2], unit_of["gk1"] // 2 + 1)
                if u >= 1:
                    pool.wait_ge(gs_made, u)
                tok = slice(a * P, a * P + P)
                q, k = gqT[:, h, tok], gkT[:, h, tok]
                for l in range(LEVELS):
                    hf = 1 << l
                    e = E[:, l + 1 - a, :].rearrange("p (b s x) -> p b s x", s=2, x=hf)
                    d = QK[:, l, :].rearrange("p (b s x) -> p b s x", s=2, x=hf)
                    for s, m in ((0, k), (1, q)):
                        pool.tensor_tensor(d[:, :, s, :], e[:, :, s, :],
                                           m.rearrange("p (b s x) -> p b s x", s=2, x=hf)[:, :, s, :], ALU.mult)
                if a == 0:
                    pool.tensor_tensor(K7, E[:, 0, :], k, ALU.mult).then_inc(gf_qk, 1)
                else:
                    pool.tensor_tensor(Q7, E[:, 7, :], q, ALU.mult).then_inc(gf_qk, 1)

            for n in range(FFN1):
                if 0 <= n - 9 < SB_H:
                    sb_mask_sp(n - 9)
                if 0 <= n - 10 < SB_H:
                    sb_mask_w(n - 10)
                if 0 <= n - 9 < 16 and (n - 9) % 2 == 0:
                    gla_factors((n - 9) // 2)
            pool.wait_ge(sb_rc, SB_H)
            pool.dma_start(res[:, :, :], x[0].rearrange("(a p) n -> p a n", p=P)).then_inc(x_again, 16)
            pool.wait_ge(gs_ready, 2 * GLA_H)
            pool.dma_start(gfin, norm_final.partition_broadcast(P)).then_inc(gfin_in, 16)
            pool.wait_ge(go_made, GLA_H)
            pool.dma_start(memx, mem_2[0].rearrange("(a p) n -> p a n", p=P)).then_inc(mem_in, 16)
            pool.dma_start(wgn[:, :, :], w_in_2[0].rearrange("(k p) n -> p k n", p=P)[:, :, 1280:1304]).then_inc(small2_in, 16)
            for half in range(2):
                pool.dma_start(w2k[:, :, half, :], cmp_w2_2[0, 0].rearrange("(f p) n -> p f n", p=P)).then_inc(small2_in, 16)
            pool.dma_start(w2v[:, :, :], cmp_w2_2[0, 1].rearrange("(f p) n -> p f n", p=P)).then_inc(small2_in, 16)
            pool.wait_ge(trlo_made, 8)
            pool.wait_ge(go_tr, GLA_H)
            pool.dma_start(cw_rows, conv_w_2[0].rearrange("k o c -> k (o c)")).then_inc(cw_in, 16)
            pool.memset(u_conv[:, :, 0:PAD], 0.0).then_inc(pad_made, 1)
            pool.wait_ge(sb_rc, SB_H)
            step(pool.memset(negtri[:, :], -1.0))
            v = negtri[:, :].rearrange("p (b x) -> p b x", b=2)
            keep(v, [[-64, 2], [0, 64]], 0, 1)
            keep(v, [[64, 2], [0, 64]], 64, -1, ALU.is_gt)
            pool.wait_ge(x3_made, TT)
            pool.memset(TMP[:, 4096:4382], 0.0).then_inc(mask2_made, 1)
            pool.wait_ge(mask2_made, 1)
            pool.affine_select(out=causal[:, P:T], in_=causal[:, P:T], compare_op=ALU.is_ge, fill=-1e30, base=0,
                               pattern=[[-1, P]], channel_multiplier=1).then_inc(mask2_made, 1)
            pool.affine_select(out=cmask, in_=cmask, compare_op=ALU.is_ge, fill=-1e30, base=-31,
                               pattern=[[P, TT], [-16, 15]], channel_multiplier=1).then_inc(mask2_made, 1)

            product = conv_product[:, :, :]

            def first_taps():
                pool.wait_ge(cw_made, 1)
                pool.wait_ge(drained[unit_of["cg1"] % 2], unit_of["cg1"] // 2 + 1)
                for f in (2, 3):
                    pool.tensor_scalar(cacc[:, f, :], u_conv[:, f, 0:T], cw[:, f, 0:1], prm[:, B_CONV + f:B_CONV + f + 1],
                                       ALU.mult, ALU.add).then_inc(taps_b, 1)
            def taps(first, last):
                for k in range(max(first, 1), min(last, 31)):
                    pool.wait_ge(taps_b, 3 * k - 1)
                    for f in range(2):
                        pool.tensor_scalar(product[:, f, :], u_conv[:, 2 + f, k:k + T], cw[:, 2 + f, k:k + 1], None,
                                           ALU.mult).then_inc(taps_b, 1)
                    pool.wait_ge(taps_b, 3 * k + 1)
                    pool.tensor_tensor(cacc[:, 2:4, :], cacc[:, 2:4, :], product, ALU.add).then_inc(taps_b, 1)

            for n in POOL_LO:
                if n == POOL_LO[0] + 5:
                    first_taps()
                pool.wait_ge(hi_made, n + 1)
                pool.tensor_tensor(wlo[:, n % RING, SHARE:2048], raw[:, n % RING, SHARE:2048],
                                   whi[:, n % RING, SHARE:2048].bitcast(F32), ALU.subtract).then_inc(lob_made, 1)
                if n >= POOL_LO[0] + 5:
                    s = n - POOL_LO[0] - 5
                    taps(2 * s, 2 * s + 2)

        @block.tensor
        def _(pe):
            def mm3(dst, a_hi, a_lo, b_hi, b_lo, start, stop):
                pe.matmul(dst, a_hi, b_hi, start=start, stop=False, skip_group_check=True)
                pe.matmul(dst, a_hi, b_lo, start=False, stop=False, skip_group_check=True)
                return pe.matmul(dst, a_lo, b_hi, start=False, stop=stop, skip_group_check=True)

            def parts(n, width):
                return [w[:, n % RING, :].rearrange("p (k n) -> p k n", n=width) for w in (whi, wlo)]

            def take(n, it=0):
                pe.wait_ge(lo_made, n + 1 + 6 * it)
                if n in POOL_LO:
                    pe.wait_ge(lob_made, n - POOL_LO[0] + 1)

            def free_unit(u):
                if u >= 2:
                    pe.wait_ge(drained[u % 2], u // 2)

            def feature_major(name, x_hi, x_lo, k0=0, kn=KT, width=CW):
                n, u = at[name], unit_of[name]
                take(n)
                w_hi, w_lo = parts(n, width)
                for f in range(width // P):
                    if f % 2 == 0:
                        free_unit(u + f // 2)
                    dst = lin(u + f // 2)[:, (f % 2) * T:(f % 2) * T + T]
                    for k in range(kn):
                        mm = mm3(dst, w_hi[:, k, f * P:(f + 1) * P], w_lo[:, k, f * P:(f + 1) * P],
                                 x_hi[:, k0 + k, :], x_lo[:, k0 + k, :], k == 0, k == kn - 1)
                mm.then_inc(chunk_used, 1)

            def token_major(name, x_hi, x_lo):
                n, u = at[name], unit_of[name]
                take(n)
                free_unit(u)
                w_hi, w_lo = parts(n, CW)
                for a in range(TT):
                    for k in range(KT):
                        mm = mm3(lin(u)[:, a * CW:(a + 1) * CW], x_hi[:, k, a * P:(a + 1) * P],
                                 x_lo[:, k, a * P:(a + 1) * P], w_hi[:, k, :], w_lo[:, k, :], k == 0, k == KT - 1)
                mm.then_inc(chunk_used, 1)

            def into_residual(n, x_hi, x_lo, stop, it=0):
                take(n, it)
                w_hi, w_lo = parts(n, D)
                for k in range(2):
                    for a in range(TT):
                        for c in range(2):
                            mm = mm3(ACC[a][:, c, :], x_hi[:, k, a * P:(a + 1) * P], x_lo[:, k, a * P:(a + 1) * P],
                                     w_hi[:, k, c * 512:(c + 1) * 512], w_lo[:, k, c * 512:(c + 1) * 512],
                                     False, stop and k == 1)
                mm.then_inc(chunk_used, 1)
                return mm

            def transposes(event, q, src):
                g = 4 * event + q
                if g >= 2:
                    pe.wait_ge(trlo_made, g - 1)
                for f in range(2):
                    for a in range(TT):
                        mm = pe.transpose(PS[:, 6 + q % 2, f * T + a * P:f * T + (a + 1) * P],
                                          src[:, a, (2 * q + f) * P:(2 * q + f + 1) * P], ident[:, :])
                mm.then_inc(tr_made, 1)

            def sb_scores(h):
                r = slice(64 * (h % 2), 64 * (h % 2) + 64)
                z = PS[:, h % 2, :]
                if h >= 2:
                    pe.wait_ge(sb_wm, h - 1)
                if h == 0:
                    pe.wait_ge(drained[unit_of["sbk1"] % 2], unit_of["sbk1"] // 2 + 1)
                    pe.wait_ge(drained[unit_of["sbk0"] % 2], unit_of["sbk0"] // 2 + 1)
                pe.matmul(z[:, 0:256], kT_sb[r, h // 2, 0:P], qT_sb[r, h // 2, :], start=True, stop=False,
                          skip_group_check=True)
                pe.matmul(z[:, 256:384], kT_sb[r, h // 2, P:T], qT_sb[r, h // 2, P:T], start=False, stop=False,
                          skip_group_check=True).then_inc(sb_z, 1)

            def sb_later(h):
                z, spv = PS[:, h % 2, :], sbt[:, h % 2, 1, :]
                if h == 0:
                    pe.wait_ge(const_made, CONSTS)
                pe.wait_ge(sb_spm, h + 1)
                pe.matmul(z[:, 0:384], negtri[:, :], spv, start=False, stop=False, skip_group_check=True)
                pe.matmul(z[:, 128:256], negone[:, :], spv[:, 256:384], start=False, stop=True,
                          skip_group_check=True).then_inc(sb_rc, 1)

            def sb_values(h):
                r = slice(64 * (h % 2), 64 * (h % 2) + 64)
                o, w = PS[r, 2, 0:256], sb_w[:, h % 2, :]
                pe.wait_ge(sb_wk, h + 1)
                if h == 0:
                    for c in ("sbv0", "sbv1"):
                        pe.wait_ge(drained[unit_of[c] % 2], unit_of[c] // 2 + 1)
                if h % 2 == 0 and h >= 2:
                    pe.wait_ge(sb_lo, h // 2)
                d = slice(h * SB_D, (h + 1) * SB_D)
                pe.matmul(o, v_sb[:, 0, d], w[:, 0:256], start=True, stop=False, skip_group_check=True)
                pe.matmul(PS[r, 2, 128:256], v_sb[:, 1, d], w[:, 256:384], start=False, stop=True,
                          skip_group_check=True).then_inc(sb_pv, 1)

            def gla_gate(a):
                pe.wait_ge(drained[0], 1)
                pe.wait_ge(gup_in, 32)
                pe.wait_ge(ident_made, 4)
                pe.matmul(PS[:, 6 + a, :], glow[:, a * P:(a + 1) * P], wup[:, :], start=True, stop=False)
                pe.matmul(PS[:, 6 + a, :], onerow, bup[:, :], start=False, stop=True).then_inc(ga_y, 1)

            def gla_sums(u):
                h, a = u // 2, u % 2
                if u == 0:
                    pe.wait_ge(ga_made, 2)
                    pe.wait_ge(const_made, CONSTS)
                if u >= 1:
                    pe.wait_ge(gs_masked, u)
                for c in range(2):
                    mm = pe.matmul(PS[:, 6 + c, :], a_ls[:, a, h * P:(h + 1) * P],
                                   decay_sum[:, a + 4 * c:a + 4 * c + 4, :], start=True, stop=True)
                mm.then_inc(gf_sum, 1)

            def gla_scores(u):
                h, a = u // 2, u % 2
                pe.wait_ge(gf_qk, u + 1)
                for l in range(LEVELS):
                    pe.matmul(PS[:, 6 + l // 4, (l % 4) * P:(l % 4) * P + P], QK[:, l, :], QK[:, l, :],
                              start=True, stop=True)
                if a == 1:
                    if h >= 1:
                        pe.wait_ge(go_lo, h)
                    pe.matmul(PS[:, 3, 0:128], K7, Q7, start=True, stop=True)
                tok = slice(a * P, a * P + P)
                pe.matmul(PS[:, 7, 384:512], gkT[:, h, tok], gqT[:, h, tok], start=True, stop=True).then_inc(gs_made, 1)

            def gla_values(h):
                pe.wait_ge(gs_ready, 2 * h + 2)
                pe.wait_ge(gs_x, h + 1)
                c = f"gv{h}"
                pe.wait_ge(drained[unit_of[c] % 2], unit_of[c] // 2 + 1)
                if h >= 1:
                    pe.wait_ge(go_lo, h)
                v = slice(h * GLA_DV, (h + 1) * GLA_DV)
                pe.matmul(PS[:, 3, 0:256], S_gla[:, 0, :], gv[:, 0, v], start=True, stop=True)
                pe.matmul(PS[:, 3, 256:512], S_gla[:, 2, :], gv[:, 0, v], start=True, stop=False)
                pe.matmul(PS[:, 3, 256:512], S_gla[:, 1, :], gv[:, 1, v], start=False, stop=True).then_inc(go_made, 1)

            def gla_turn(h):
                pe.wait_ge(go_norm, h + 1)
                for f in range(2):
                    for a in range(TT):
                        mm = pe.transpose(PS[:, 3, f * T + a * P:f * T + (a + 1) * P],
                                          gsil[:, a, h * GLA_DV + f * P:h * GLA_DV + (f + 1) * P], ident[:, :])
                mm.then_inc(go_tr, 1)

            pe.wait_ge(ident_made, 4)
            pe.wait_ge(prm_in, 16 * PRMS)
            pe.transpose(PS[:, 5, 0:92], prm_rows, ident[0:92, 0:92]).then_inc(prm_tr, 1)
            pe.wait_ge(xn_made, TT)
            for q in range(4):
                transposes(0, q, xn)
            pe.wait_ge(trlo_made, 4)
            pe.wait_ge(prm_made, 1)

            for n in range(at["projs0"]):
                name = list(at)[n]
                if name[:-1] in ("sbv", "gv", "gout"):
                    token_major(name, hT_hi, hT_lo)
                else:
                    feature_major(name, hT_hi, hT_lo, width=P if name == "low" else CW)
                if n == 1:
                    gla_gate(0)
                    gla_gate(1)
                if 0 <= n - 9 < SB_H:
                    sb_scores(n - 9)
                if 0 <= n - 10 < SB_H:
                    sb_later(n - 10)
                if 0 <= n - 11 < SB_H:
                    sb_values(n - 11)
                if 0 <= n - 10 < 16 and (n - 10) % 2 == 0:
                    gla_scores((n - 10) // 2)
                if 0 <= n - 9 < 16 and (n - 9) % 2 == 0:
                    gla_sums((n - 9) // 2)
                if 0 <= n - 15 < 12 and (n - 15) % 4 == 0:
                    gla_turn((n - 15) // 4)
                if 0 <= n - 13 < 16 and (n - 13) % 4 == 0:
                    gla_values((n - 13) // 4)
            pe.wait_ge(sb_lo, 4)
            feature_major("projs0", oT_hi, oT_lo, 0, 4, 512)
            gla_turn(3)
            feature_major("projs1", oT_hi, oT_lo, 0, 4, 512)
            pe.wait_ge(go_lo, GLA_H)
            pe.wait_ge(x_again, 16)
            for a in range(TT):
                for c in range(2):
                    pe.matmul(ACC[a][:, c, :], ident[:, :], res[:, a, c * 512:(c + 1) * 512], start=True, stop=False,
                              skip_group_check=True)
            for c in range(4):
                feature_major(f"projg{c}", oT_hi, oT_lo, 4, KT)
            for c in range(4):
                pe.wait_ge(mix_lo, c + 1)
                mm = into_residual(at[f"wout{c}"], hT_hi[:, 2 * c:2 * c + 2, :], hT_lo[:, 2 * c:2 * c + 2, :], c == 3)
                if c == 0:
                    pe.wait_ge(xn_made, 2 * TT)
                    transposes(1, 0, memx)
                    transposes(1, 1, memx)
                if c == 1:
                    transposes(1, 2, memx)
                    transposes(1, 3, memx)
            pe.wait_ge(trlo_made, 8)
            for c in range(2):
                feature_major(f"km{c}", oT_hi, oT_lo)
            pe.wait_ge(xn_made, 3 * TT)
            for q in range(4):
                transposes(2, q, xn)
            pe.wait_ge(trlo_made, 12)

            def expand(n, j, it=0):
                take(n, it)
                w_hi, w_lo = parts(n, CW)
                for c in range(2):
                    for k in range(KT):
                        mm = mm3(PS[:, 4 + j, c * T:(c + 1) * T], w_hi[:, k, c * P:(c + 1) * P],
                                 w_lo[:, k, c * P:(c + 1) * P], hT_hi[:, k, :], hT_lo[:, k, :], k == 0, k == KT - 1)
                mm.then_inc(chunk_used, 1)

            def contract(n, f, j, it=0, last=False):
                pe.wait_ge(h1_lo, f + 1 + 3 * it)
                return into_residual(n, aT_hi[:, j], aT_lo[:, j], last, it)

            for b in range(2):
                pe.wait_ge(drained[b], (units_before_ffn1 - b + 1) // 2)
            expand(FFN1, 0)
            with pe.Fori(0, (F1 - 1) // 3) as it:
                for j in range(3):
                    expand(FFN1 + 1 + 2 * j, (j + 1) % 3, it)
                    contract(FFN1 + 2 + 2 * j, j, j, it)
            contract(after_ffn1 - 1, F1 - 1, 0, last=True)

            pe.wait_ge(cw_in, 16)
            for f in range(4):
                mm = pe.transpose(PS[:, 7, 31 * f:31 * f + 31], cw_rows[:, f * P:(f + 1) * P], ident[0:31, 0:31])
            mm.then_inc(cw_tr, 1)
            for c in range(2):
                token_major(f"vm{c}", oT_hi, oT_lo)
            pe.wait_ge(cw_made, 1)
            pe.wait_ge(xn_made, 4 * TT)
            for q in range(4):
                transposes(3, q, xn)
            pe.wait_ge(trlo_made, 16)

            def key_and_value(name):
                n, u = at[name], unit_of[name]
                take(n)
                free_unit(u)
                w_hi, w_lo = parts(n, CW)
                for k in range(KT):
                    mm3(lin(u)[:, 0:T], w_hi[:, k, 0:P], w_lo[:, k, 0:P], hT_hi[:, k, :], hT_lo[:, k, :],
                        k == 0, k == KT - 1)
                for a in range(TT):
                    for k in range(KT):
                        mm = mm3(lin(u)[:, T + a * P:T + (a + 1) * P], hT_hi[:, k, a * P:(a + 1) * P],
                                 hT_lo[:, k, a * P:(a + 1) * P], w_hi[:, k, P:CW], w_lo[:, k, P:CW],
                                 k == 0, k == KT - 1)
                mm.then_inc(chunk_used, 1)

            def compress(b, c):
                name = f"{'wk' if b == 0 else 'wv'}{c}"
                n, u = at[name], unit_of[name]
                take(n)
                if c == 0:
                    free_unit(u)
                    pe.wait_ge(blk_lod, b + 1)
                w_hi, w_lo = parts(n, CW)
                for f in range(2):
                    for m in range(8):
                        mm = mm3(lin(u)[:, 30 * f:30 * f + 30], w_hi[:, m, f * P:(f + 1) * P], w_lo[:, m, f * P:(f + 1) * P],
                                 blk_hi[b][:, 8 * c + m, :], blk_lo[b][:, 8 * c + m, :],
                                 (c, f, m) == (0, 0, 0), (c, m) == (1, 7))
                mm.then_inc(chunk_used, 1)

            def head_sums(e):
                src, width, size, gain = FN[e][0:4]
                pe.wait_ge(fn_sq, e + 1)
                if e >= 1:
                    pe.wait_ge(fn_ln, e)
                    pe.wait_ge(fn_var, e)
                if e == 0:
                    pe.wait_ge(const_made, CONSTS + 3)
                pe.matmul(PS[:, 7, 0:width], negone[:, :] if size == P else negtri[:, :], scratch(e)[0],
                          start=True, stop=True).then_inc(fn_sum, 1)

            def att_scores(i):
                kind, a, g = ATT[i]
                if i >= 1:
                    pe.wait_ge(att_e, 4 * i)
                if i == 0:
                    pe.wait_ge(fn_made, 4)
                    for c in ("vm0", "vm1"):
                        pe.wait_ge(drained[unit_of[c] % 2], unit_of[c] // 2 + 1)
                if i == 2:
                    pe.wait_ge(fn_made, 8)
                    pe.wait_ge(kd_made, 2)
                if i == 4:
                    pe.wait_ge(fn_made, 9)
                tok = slice(a * P, (a + 1) * P)
                for h in range(4):
                    if kind == "m":
                        mm = pe.matmul(PS[:, h // 2, (h % 2) * T:(h % 2) * T + T], qm[:, h, tok], kmT[:, h, :],
                                       start=True, stop=True)
                        continue
                    r = slice(64 * (h % 2), 64 * (h % 2) + 64)
                    q = qn[r, 2 * g + h // 2, tok]
                    L = 15 if kind == "c" else P * (a + 1)
                    k = kcT[r, 15 * g:15 * g + 15] if kind == "c" else kdup[kind][r, g, 0:L]
                    mm = pe.matmul(PS[:, h % 2, h // 2 * L:(h // 2 + 1) * L], q, k, start=True, stop=True)
                mm.then_inc(att_s, 1)

            def att_turn(i):
                kind, a, g = ATT[i]
                pe.wait_ge(att_p, 4 * i + 4)
                if i >= 1:
                    pe.wait_ge(att_pt, i)
                L = 15 if kind == "c" else P
                for s in range(key_tiles(i)):
                    for h in range(4):
                        mm = pe.transpose(PS[0:L, 2 + s, h * P:(h + 1) * P],
                                          pbuf[:, i % 2, (h * key_tiles(i) + s) * L:(h * key_tiles(i) + s + 1) * L],
                                          ident[:, :])
                mm.then_inc(att_t, 1)

            def att_values(i):
                kind, a, g = ATT[i]
                pe.wait_ge(att_pt, i + 1)
                first = kind in "ms"
                if first and i >= 1:
                    pe.wait_ge(att_lo, group_of(i))
                if kind == "m":
                    for h in range(4):
                        for s in range(2):
                            mm = pe.matmul(PS[:, 6, h * P:(h + 1) * P], vm[:, s, h * P:(h + 1) * P],
                                           pT[:, i % 2, (s * 4 + h) * P:(s * 4 + h + 1) * P], start=s == 0, stop=s == 1)
                elif kind == "c":
                    pe.wait_ge(vc_made, 1)
                    mm = pe.matmul(PS[0:64, 6, :], vc[:, g, :], pT[0:15, i % 2, 0:512], start=False, stop=True,
                                   skip_group_check=True)
                else:
                    for s in range(key_tiles(i)):
                        mm = pe.matmul(PS[0:64, 6, :], vn[kind][:, s, 64 * g:64 * g + 64],
                                       pT[:, i % 2, s * 512:(s + 1) * 512], start=kind == "s" and s == 0, stop=False,
                                       skip_group_check=True)
                mm.then_inc(att_o, 1)

            B2 = at["ca0"]
            for s in range(FFN2 - B2 - 4):
                name = list(at)[B2 + s - 2 * F1]
                if name in ("ksvs", "kwvw"):
                    key_and_value(name)
                elif name[:2] in ("wk", "wv"):
                    compress(int(name[1] == "v"), int(name[2]))
                elif name.startswith("o"):
                    br = "mcn".index(name[2])
                    if name[3] == "0":
                        if br == 0:
                            pe.wait_ge(att_lo, 2)
                        elif br == 1:
                            pe.wait_ge(cv_lo, 1)
                        else:
                            pe.wait_ge(att_lo, 6)
                    feature_major(name, oT_hi, oT_lo, (8, 4, 0)[br], 4, 512)
                else:
                    feature_major(name, hT_hi, hT_lo)
                if s == 0:
                    pe.wait_ge(small2_in, 64)
                    for a in range(TT):
                        for k in range(KT):
                            for w, x_ in enumerate((hT_hi, hT_lo)):
                                mm = pe.matmul(PS[:, 7, 24 * a:24 * a + 24], x_[:, k, a * P:(a + 1) * P].bitcast(F32),
                                               wgn[:, k, :], start=(k, w) == (0, 0), stop=(k, w) == (KT - 1, 1))
                    mm.then_inc(gn_sum, 1)
                if s in FN_AT:
                    if s == FN_AT[0]:
                        pe.wait_ge(gn_made, 1)
                    head_sums(FN_AT.index(s))
                if s - 9 in (3, 4):
                    att_values(s - 12)
                if s - 9 in (2, 3):
                    att_turn(s - 11)
                if s - 9 in (0, 1):
                    att_scores(s - 9)
                if 0 <= s - 18 < 12:
                    att_values(s - 16)
                if 0 <= s - 17 < 12:
                    att_turn(s - 15)
                if 0 <= s - 15 < 12:
                    att_scores(s - 13)
                if s == 15:
                    pe.wait_ge(h_made, 1)
                    pe.wait_ge(fn_made, 8)
                    for f in range(2):
                        mm = pe.matmul(PS[:, 7, 0:30], w2k[:, f].rearrange("p b n -> p (b n)"), hid[0][:, 30 * f:30 * f + 30],
                                       start=f == 0, stop=f == 1)
                    mm.then_inc(kc_sum, 1)
                if s == 17:
                    pe.wait_ge(fn_made, 9)
                    pe.wait_ge(h_made, 2)
                    for g in range(2):
                        for f in range(2):
                            mm = pe.matmul(PS[0:15, 7, 64 * g:64 * g + 64], hid[1][:, 30 * f + 15 * g:30 * f + 15 * g + 15],
                                           w2v[:, f, :], start=f == 0, stop=f == 1)
                    mm.then_inc(kc_sum, 1)
                if s == 20:
                    pe.wait_ge(vc_made, 1)
                    pe.wait_ge(taps, 62)
                    pe.wait_ge(taps_b, 92)
                    for f in range(4):
                        mm = pe.matmul(PS[:, 7, 0:T], negone[:, :], cacc[:, f, :], start=f == 0, stop=f == 3)
                    mm.then_inc(cv_mean, 1)
                if s == 21:
                    pe.wait_ge(cv_sq, 1)
                    for f in range(4):
                        mm = pe.matmul(PS[:, 7, 0:T], negone[:, :], u_flat[:, f * T:(f + 1) * T], start=f == 0, stop=f == 3)
                    mm.then_inc(cv_mean, 1)
            for a in range(TT):
                for c in range(2):
                    pe.matmul(ACC[a][:, c, :], ident[:, :], res[:, a, c * 512:(c + 1) * 512], start=True, stop=False,
                              skip_group_check=True)
            for c in range(4):
                pe.wait_ge(mlo_made, c + 1)
                into_residual(at[f"xout{c}"], hT_hi[:, 2 * c:2 * c + 2, :], hT_lo[:, 2 * c:2 * c + 2, :], c == 3)
            pe.wait_ge(xn_made, 5 * TT)
            for q in range(4):
                transposes(4, q, xn)
            pe.wait_ge(trlo_made, 20)
            for b in range(2):
                pe.wait_ge(drained[b], (units - b + 1) // 2)

            def gate_or_up(n, bank, it=0):
                take(n, it)
                w_hi, w_lo = parts(n, CW)
                for c in range(2):
                    for k in range(KT):
                        mm = mm3(PS[:, bank, c * T:(c + 1) * T], w_hi[:, k, c * P:(c + 1) * P],
                                 w_lo[:, k, c * P:(c + 1) * P], hT_hi[:, k, :], hT_lo[:, k, :], k == 0, k == KT - 1)
                mm.then_inc(chunk_used, 1)

            def down(n, f, j, it=0, last=False):
                pe.wait_ge(s_lo, f + 1 + 2 * it)
                into_residual(n, aT_hi[:, j], aT_lo[:, j], last, it)

            def step2(j, it, f):
                gate_or_up(FFN2 + 2 + 3 * f, 4 + 2 * ((j + 1) % 2), it)
                gate_or_up(FFN2 + 3 + 3 * f, 5 + 2 * ((j + 1) % 2), it)
                down(FFN2 + 4 + 3 * f, f, j, it)

            gate_or_up(FFN2, 4)
            gate_or_up(FFN2 + 1, 5)
            with pe.Fori(0, 4) as it:
                for j in range(2):
                    step2(j, it, j)
            for f in (8, 9):
                step2(f % 2, 0, f)
            down(FFN2 + 32, F2 - 1, 0, last=True)

        @block.scalar
        def _(act):
            small = [(slice(G_MIX, G_MIX + 8), norm_mix[0].rearrange("(r c) -> r c", c=P)),
                     (slice(G_MLP, G_MLP + 8), norm_mlp[0].rearrange("(r c) -> r c", c=P)),
                     (slice(G_MIX2, G_MIX2 + 8), norm_mix_2[0].rearrange("(r c) -> r c", c=P)),
                     (slice(G_MEM, G_MEM + 8), norm_mem_2[0].rearrange("(r c) -> r c", c=P)),
                     (slice(G_FFN, G_FFN + 8), norm_ffn_2[0].rearrange("(r c) -> r c", c=P)),
                     (slice(G_GLA, G_GLA + 2), gla_norm[0].rearrange("(r c) -> r c", c=P)),
                     (slice(B_CONV, B_CONV + 4), conv_b_2[0].rearrange("(r c) -> r c", c=P)),
                     (slice(LN_G, LN_G + 4), conv_ln_g_2[0].rearrange("(r c) -> r c", c=P)),
                     (slice(LN_B, LN_B + 4), conv_ln_b_2[0].rearrange("(r c) -> r c", c=P)),
                     (slice(G_MQK, G_MQK + 2), mem_qk_norm_2[0]),
                     (slice(POS, POS + 32), cmp_pos_2[0].rearrange("b (m l) d -> (b m) (l d)", l=2))]
            act.add_instruction(mybir.InstLoadActFuncSet(act_func_set_id=6, name=nc.get_next_instruction_name(), engine=mybir.EngineType.Activation))
            for r, src in small:
                act.dma_start(prm_rows[r, :], src).then_inc(prm_in, 16)
            for half in range(2):
                act.dma_start(prm_rows[G_NSA:G_NSA + 4, 64 * half:64 * half + 64], nsa_qk_norm_2[0]).then_inc(prm_in, 16)
            act.dma_start(wup[:, :], w_gate_up[0]).then_inc(gup_in, 16)
            act.dma_start(bup[:, :], b_gate_up).then_inc(gup_in, 16)

            links = [0]

            def link(ins):
                links[0] += 1
                ins.then_inc(act_link, 1)
                act.wait_ge(act_link, links[0])

            def split_hi(n, it=0, width=2048):
                act.wait_ge(landed[n % RING], 16 * (n // RING + 1) + 32 * it)
                if n >= RING:
                    act.wait_ge(chunk_used, n - RING + 1 + 6 * it)
                act.copy(whi[:, n % RING, 0:width], raw[:, n % RING, 0:width]).then_inc(hi_made, 1)

            def squares(event, src, junk):
                for a in range(TT):
                    if a == 1 and event == 1:
                        act.wait_ge(ssq_made, TT * event + 1)
                    act.activation(junk[a], src[a], ACT.Square,
                                   accum_out=stat[:, event, a:a + 1]).then_inc(ssq_made, 1)

            def root(count, st=None):
                st = stat[:, count if count < 4 else 4, :] if st is None else st
                act.wait_ge(var_made, count + 1)
                act.activation(st[:, 4:6], st[:, 2:4], ACT.Ln).then_inc(ln_made, 1)
                act.wait_ge(ln_made, count + 1)
                act.activation(st[:, 4:6], st[:, 4:6], ACT.Exp, scale=-0.5).then_inc(exp_made, 1)

            def turned_hi(event, dst, gain):
                for q in range(4):
                    act.wait_ge(tr_made, 4 * event + q + 1)
                    for f in range(2):
                        act.activation(dst[:, 2 * q + f, :], PS[:, 6 + q % 2, f * T:(f + 1) * T], ACT.Copy,
                                       scale=prm[:, gain + 2 * q + f:gain + 2 * q + f + 1]).then_inc(trhi_made, 1)

            def evac(name):
                n, u = at[name], unit_of[name]
                kind, c = name[:-1], name[-1]
                act.wait_ge(chunk_used, n + 1)
                src = lin(u)
                two = src.rearrange("p (f t) -> p f t", f=2)
                if name == "low":
                    act.copy(glow[:, :], PS[0:RANK, 4 + u % 2, 0:T]).then_inc(drained[u % 2], 1)
                    return
                c = int(c)
                if kind in ("sbq", "gq"):
                    dst, scale = (qT_sb, SB_D ** -0.5) if kind == "sbq" else (gqT, GLA_DK ** -0.5)
                    act.mul(dst[:, 2 * c:2 * c + 2, :], two, scale).then_inc(drained[u % 2], 1)
                elif kind in ("sbk", "gk"):
                    act.copy((kT_sb if kind == "sbk" else gkT)[:, 2 * c:2 * c + 2, :], two).then_inc(drained[u % 2], 1)
                elif kind in ("sbv", "gv"):
                    act.copy((v_sb if kind == "sbv" else gv)[:, :, c * CW:(c + 1) * CW], two).then_inc(drained[u % 2], 1)
                elif kind in ("gout", "gates", "gateg"):
                    sigmoid_a(name)

            def sigmoid_a(name):
                t, src = relu[:, unit_of[name] % 2, :], lin(unit_of[name])
                link(act.activation(t, src, ACT.Abs))
                link(act.activation(t, t, ACT.Exp, scale=-1.0))
                act.activation(t, t, ACT.Ln, bias=1.0).then_inc(sg_ln, 1)

            def evac_end(name):
                kind, c, u = name[:-1], name[-1], unit_of[name]
                if kind in ("gout", "gates", "gateg"):
                    t = relu[:, u % 2, :]
                    act.wait_ge(sg_min, SIG.index(name) + 1)
                    if kind == "gout":
                        act.activation(t, t, ACT.Exp).then_inc(sg_exp, 1)
                        return
                    dst = (gate_s if kind == "gates" else gate_g)[:, 2 * int(c):2 * int(c) + 2, :]
                    act.activation(dst, t.rearrange("p (f t) -> p f t", f=2), ACT.Exp).then_inc(drained[u % 2], 1)

            def sb_soft(h):
                z, t = PS[:, h % 2, 0:384], sbt[:, h % 2, 0, :]
                act.wait_ge(sb_z, h + 1)
                if h >= 2:
                    act.wait_ge(sb_sp, h - 1)
                act.activation(t, z, ACT.Abs).then_inc(sb_abs, 1)
                act.wait_ge(sb_abs, h + 1)
                act.activation(t, t, ACT.Exp, scale=-1.0).then_inc(sb_e, 1)
                act.wait_ge(sb_e, h + 1)
                act.activation(t, t, ACT.Ln, bias=1.0).then_inc(sb_l, 1)

            def sb_exp(h):
                act.wait_ge(sb_rc, h + 1)
                if h >= 2:
                    act.wait_ge(sb_pv, h - 1)
                act.activation(sb_w[:, h % 2, :], PS[:, h % 2, 0:384], ACT.Exp).then_inc(sb_wm, 1)

            def sb_out(j):
                act.wait_ge(sb_pv, 2 * j + 2)
                act.copy(oT_hi[:, j, :], PS[:, 2, 0:256]).then_inc(sb_hi, 1)

            def gla_gate(a):
                act.wait_ge(ga_y, a + 1)
                t = relu[:, a, :]
                act.activation(t, PS[:, 6 + a, :], ACT.Abs).then_inc(ga_abs, 1)
                act.wait_ge(ga_abs, a + 1)
                act.activation(t, t, ACT.Exp, scale=-1.0).then_inc(ga_e, 1)
                act.wait_ge(ga_e, a + 1)
                act.activation(t, t, ACT.Ln, bias=1.0).then_inc(ga_l, 1)

            def gla_exp(u):
                act.wait_ge(gf_sum, u + 1)
                if u >= 1:
                    act.wait_ge(gs_ready, u)
                act.activation(E.rearrange("p l t -> p (l t)"), PS[:, 6:8, :].rearrange("p b n -> p (b n)"),
                               ACT.Exp, scale=1.0 / 16).then_inc(gf_exp, 1)

            def gla_norm_act(h):
                act.wait_ge(go_made, h + 1)
                for a in range(TT):
                    if 2 * h + a >= 1:
                        act.wait_ge(go_ssq, 2 * h + a)
                    act.activation(junk_g, PS[:, 3, a * 256:(a + 1) * 256], ACT.Square,
                                   accum_out=gstat[:, h, a:a + 1]).then_inc(go_ssq, 1)
                act.wait_ge(go_var, h + 1)
                act.activation(gstat[:, h, 4:6], gstat[:, h, 2:4], ACT.Ln).then_inc(go_ln, 1)
                act.wait_ge(go_ln, h + 1)
                act.activation(gstat[:, h, 4:6], gstat[:, h, 4:6], ACT.Exp, scale=-0.5).then_inc(go_exp, 1)

            def gla_out(h):
                act.wait_ge(go_tr, h + 1)
                for f in range(2):
                    act.activation(oT_hi[:, 4 + 2 * h + f, :], PS[:, 3, f * T:(f + 1) * T], ACT.Copy,
                                   scale=prm[:, G_GLA + f:G_GLA + f + 1]).then_inc(go_hi, 1)

            act.wait_ge(x_in, 16)
            squares(0, [res[:, a, :] for a in range(TT)], [xn[:, a, :] for a in range(TT)])
            act.wait_ge(prm_tr, 1)
            act.copy(prm[:, :], PS[:, 5, 0:92]).then_inc(prm_made, 1)
            root(0)
            split_hi(0, width=1024)
            split_hi(1)
            act.wait_ge(prm_made, 1)
            turned_hi(0, hT_hi, G_MIX)
            split_hi(2)
            for n in range(at["projs0"]):
                name = list(at)[n]
                evac(name)
                split_hi(n + RING)
                evac_end(name)
                if n == 1:
                    gla_gate(0)
                    gla_gate(1)
                if 0 <= n - 9 < SB_H:
                    sb_soft(n - 9)
                if 0 <= n - 10 < SB_H:
                    sb_exp(n - 10)
                if 0 <= n - 12 < SB_H and n % 2 == 0:
                    sb_out((n - 12) // 2)
                if 0 <= n - 9 < 16 and (n - 9) % 2 == 0:
                    gla_exp((n - 9) // 2)
                if 0 <= n - 15 < 12 and (n - 15) % 4 == 0:
                    gla_out((n - 15) // 4)
                if 0 <= n - 13 < 16 and (n - 13) % 4 == 0:
                    gla_norm_act((n - 13) // 4)
            p0 = at["projs0"]
            split_hi(p0 + 3)
            gla_out(3)
            split_hi(p0 + 4)
            act.wait_ge(mem_in, 16)
            act.wait_ge(gs_masked, 8)
            squares(1, [memx[:, a, :] for a in range(TT)],
                    [PS[:, 6:8, :].rearrange("p b n -> p (b n)")] * 2)
            for c in range(4):
                split_hi(p0 + 5 + c)
                act.wait_ge(mix_b, c + 1)
                act.copy(hT_hi[:, 2 * c:2 * c + 2, :], gate_s[:, 2 * c:2 * c + 2, :]).then_inc(mix_hi, 1)
                if c == 0:
                    root(1)
            for c in range(3):
                split_hi(p0 + 9 + c)
                if c == 0:
                    act.wait_ge(chunk_used, at["projg3"] + 1)
                    turned_hi(1, oT_hi, G_MEM)
            act.wait_ge(chunk_used, at["wout3"] + 1)
            squares(2, ACC_FLAT, [xn[:, a, :] for a in range(TT)])
            root(2)
            split_hi(FFN1)

            def km_out(c):
                act.wait_ge(chunk_used, at[f"km{c}"] + 1)
                act.copy(kmT[:, 2 * c:2 * c + 2, :], lin(unit_of[f"km{c}"]).rearrange("p (f t) -> p f t", f=2)) \
                   .then_inc(drained[unit_of[f"km{c}"] % 2], 1)

            km_out(0)
            split_hi(FFN1 + 1)
            km_out(1)
            split_hi(FFN1 + 2)
            turned_hi(2, hT_hi, G_MLP)

            def relu_square(f, j, it=0):
                act.wait_ge(chunk_used, (FFN1 + 2 * f if f else FFN1 + 1) + 6 * it)
                act.activation(relu[:, j, :], PS[:, 4 + j, :], ACT.Relu).then_inc(h1_relu, 1)
                act.wait_ge(h1_relu, f + 1 + 3 * it)
                act.activation(aT_hi[:, j].rearrange("p a t -> p (a t)"), relu[:, j, :], ACT.Square).then_inc(h1_hi, 1)

            relu_square(0, 0)
            split_hi(FFN1 + 3)
            with act.Fori(0, (F1 - 1) // 3) as it:
                for j in range(3):
                    relu_square(j + 1, (j + 1) % 3, it)
                    split_hi(FFN1 + 4 + 2 * j, it)
                    split_hi(FFN1 + 5 + 2 * j, it)
            act.wait_ge(chunk_used, after_ffn1)
            squares(3, ACC_FLAT, [xn[:, a, :] for a in range(TT)])
            root(3)
            split_hi(after_ffn1 + 2)
            act.wait_ge(x3_made, TT)
            for a in range(TT):
                act.activation(xn[:, a, :], res[:, a, :], ACT.Square, accum_out=stat[:, 5, a:a + 1]).then_inc(ssq_made, 1)
            root(4, stat[:, 5, :])
            act.wait_ge(cw_tr, 1)
            act.copy(cw[:, :, :].rearrange("p f k -> p (f k)"), PS[:, 7, 0:124]).then_inc(cw_made, 1)

            def evac2(name):
                n, u = at[name], unit_of[name]
                act.wait_ge(chunk_used, n + 1)
                done = drained[u % 2]
                two = lin(u).rearrange("p (f t) -> p f t", f=2)
                if name[:2] == "vm":
                    c = int(name[2])
                    act.copy(vm[:, :, c * CW:(c + 1) * CW], two).then_inc(done, 1)
                elif name[:2] == "ca":
                    c = int(name[2])
                    if c == 0:
                        act.wait_ge(pad_made, 1)
                    act.copy(u_conv[:, 2 * c:2 * c + 2, PAD:PAD + T], two).then_inc(done, 1)
                elif name[:2] == "qm" or name in ("q0", "q1"):
                    c = int(name[-1])
                    act.copy((qm if name[:2] == "qm" else qn)[:, 2 * c:2 * c + 2, :], two).then_inc(done, 1)
                elif name == "kcvc":
                    for b in range(2):
                        for g in range(2):
                            src = lin(u)[64 * g:64 * g + 64, b * T:(b + 1) * T]
                            act.copy(Z[b][0:64, g, :], src).then_inc(z_made, 1)
                            act.copy(Z[b][64:128, g, 0:T - 1], src[:, 1:T]).then_inc(done if (b, g) == (1, 1) else z_made, 1)
                elif name in ("ksvs", "kwvw"):
                    kind = name[1]
                    act.copy(kdup[kind][:, 0, :], lin(u)[:, 0:T]).then_inc(raw_made, 1)
                    act.copy(vn[kind], lin(u)[:, T:2 * T].rearrange("p (a n) -> p a n", a=TT)).then_inc(done, 1)
                elif name in ("wk1", "wv1"):
                    b = int(name[1] == "v")
                    act.copy(hid[b], lin(u)[:, 0:60]).then_inc(done, 1)
                elif name[0] == "g" or name[:2] == "cg":
                    sigmoid_a(name)

            def evac2_end(name):
                if name[0] == "g" or name[:2] == "cg":
                    i, u = SIG.index(name), unit_of[name]
                    t = relu[:, u % 2, :]
                    act.wait_ge(sg_min, i + 1)
                    if name[0] == "c":
                        act.activation(t, t, ACT.Exp).then_inc(sg_exp, 1)
                        return
                    c = int(name[2])
                    if name == "gn0":
                        act.wait_ge(merged, 4)
                    dst = (Mg if name[1] == "m" else G)[:, 2 * c:2 * c + 2, :]
                    act.activation(dst, t.rearrange("p (f t) -> p f t", f=2), ACT.Exp).then_inc(drained[u % 2], 1)

            def head_squares(e):
                src, width, size, gain = FN[e]
                if e >= 2:
                    act.wait_ge(fn_made, e - 1)
                if e == 7:
                    act.wait_ge(att_s, 2)
                dst = scratch(e)[0]
                if width == 512:
                    dst = dst.rearrange("p (f t) -> p f t", f=2)
                for n in FN_WAIT[e]:
                    act.wait_ge(drained[unit_of[n] % 2], unit_of[n] // 2 + 1)
                if e in (4, 5):
                    act.wait_ge(raw_made, e - 3)
                if e == 8:
                    act.wait_ge(kc_raw, 1)
                act.activation(dst, src, ACT.Square).then_inc(fn_sq, 1)

            def head_root(e):
                width, size = FN[e][1:3]
                act.wait_ge(fn_sum, e + 1)
                if e >= 1:
                    act.wait_ge(fn_made, e)
                act.activation(fy[:, 0:width], PS[:, 7, 0:width], ACT.Ln, scale=-1.0 / size,
                               bias=eps[:, :]).then_inc(fn_ln, 1)
                act.wait_ge(fn_ln, e + 1)
                act.activation(fy[:, 0:width], fy[:, 0:width], ACT.Exp, scale=-0.5).then_inc(fn_exp, 1)

            def keys_twice(e):
                k = kdup["sw"[e - 4]]
                act.wait_ge(fn_made, e + 1)
                act.copy(k[64:128, 0, :], k[0:64, 0, :])
                act.copy(k[0:64, 1, :], k[64:128, 1, :]).then_inc(kd_made, 1)

            def att_exp(i):
                kind, a, g = ATT[i]
                act.wait_ge(att_max, i + 1)
                if i >= 2:
                    act.wait_ge(att_t, i - 1)
                L = {"m": T, "c": 15}.get(kind, P * (a + 1))
                for h in range(4):
                    p = pbuf[:, i % 2, h * L:(h + 1) * L]
                    src = PS[:, h // 2, (h % 2) * T:(h % 2) * T + T] if kind == "m" else p
                    act.activation(p, src, ACT.Exp, bias=amax[:, i, h:h + 1],
                                   scale=(P if kind == "m" else 64) ** -0.5,
                                   accum_out=aden[:, i, h:h + 1]).then_inc(att_e, 1)

            def att_evac(i):
                kind, a, g = ATT[i]
                act.wait_ge(att_t, i + 1)
                if i >= 2:
                    act.wait_ge(att_o, i - 1)
                L, n = 15 if kind == "c" else P, 512 * key_tiles(i)
                act.copy(pT[0:L, i % 2, 0:n], PS[0:L, 2:4, :].rearrange("p b n -> p (b n)")[:, 0:n]).then_inc(att_pt, 1)

            def att_out(i):
                kind, a, g = ATT[i]
                tok = slice(a * P, (a + 1) * P)
                act.wait_ge(att_o, i + 1)
                if kind == "m":
                    act.copy(oT_hi[:, 8:12, tok], PS[:, 6, :].rearrange("p (h t) -> p h t", h=4)).then_inc(att_hi, 1)
                    return
                src = PS[0:64, 6, :].rearrange("p (h e t) -> p e h t", h=2, e=2)
                for e in range(2):
                    ins = act.copy(oT_hi[64 * e:64 * e + 64, 2 * g:2 * g + 2, tok], src[:, e])
                ins.then_inc(att_hi, 1)

            V1 = at["vm0"]
            for n in range(V1, FFN2 - 4):
                name, s = list(at)[n - 2 * F1], n - at["ca0"]
                if name[0] != "o" and name not in ("wk0", "wv0"):
                    evac2(name)
                if s + 1 in FN_AT[:8]:
                    head_squares(FN_AT.index(s + 1))
                if s in FN_AT:
                    head_root(FN_AT.index(s))
                if n + RING < FFN2 + 33:
                    split_hi(n + RING)
                evac2_end(name)
                if name == "vm1":
                    turned_hi(3, hT_hi, G_MIX2)
                if s == 0:
                    act.wait_ge(gn_clip, 1)
                    act.activation(gn24, gn24, ACT.Exp, scale=-1.0).then_inc(gn_exp, 1)
                if s in FN_AT[4:6]:
                    keys_twice(FN_AT.index(s))
                if name == "qm0":
                    for b in range(2):
                        act.wait_ge(blk_made, 4 * b + 4)
                        act.copy(blk_hi[b], blk[b]).then_inc(blk_hid, 1)
                if name in ("wk1", "wv1"):
                    b = int(name[1] == "v")
                    act.wait_ge(h_arg, b + 1)
                    act.activation(hwork, hwork, ACT.Exp, scale=-2 * (2 / np.pi) ** 0.5).then_inc(h_exp, 1)
                if s == 15:
                    act.wait_ge(kc_sum, 1)
                    act.copy(kcT, PS[:, 7, 0:30]).then_inc(kc_raw, 1)
                    head_squares(8)
                if s == 17:
                    act.wait_ge(kc_sum, 2)
                    act.copy(vc.rearrange("p g n -> p (g n)"), PS[0:15, 7, 0:128]).then_inc(vc_made, 1)
                if s - 9 in (3, 4):
                    att_out(s - 12)
                if s - 9 in (2, 3):
                    att_evac(s - 11)
                if s - 9 in (0, 1):
                    att_exp(s - 9)
                if 0 <= s - 18 < 12 and ATT[s - 16][0] == "c":
                    att_out(s - 16)
                if 0 <= s - 17 < 12:
                    att_evac(s - 15)
                if 0 <= s - 15 < 12:
                    att_exp(s - 13)
                if s == 20:
                    act.wait_ge(cv_mid, 1)
                    act.activation(u_flat, cacc_flat, ACT.Square).then_inc(cv_sq, 1)
                if s == 21:
                    act.wait_ge(cv_var, 1)
                    act.activation(u_flat[:, T:2 * T], u_flat[:, 0:T], ACT.Ln).then_inc(cv_ln, 1)
                    act.wait_ge(cv_ln, 1)
                    act.activation(u_flat[:, T:2 * T], u_flat[:, T:2 * T], ACT.Exp, scale=-0.5).then_inc(cv_exp, 1)
                    act.wait_ge(cv_y, 1)
                    for f in range(4):
                        act.activation(cacc[:, f, :], cacc[:, f, :], ACT.Identity, scale=prm[:, LN_G + f:LN_G + f + 1],
                                       bias=prm[:, LN_B + f:LN_B + f + 1]).then_inc(cv_lin, 1)
                if s == 22:
                    act.wait_ge(cv_lin, 4)
                    act.activation(u_flat, cacc_flat, ACT.Abs).then_inc(cv_abs, 1)
                    act.wait_ge(cv_abs, 1)
                    link(act.activation(u_flat, u_flat, ACT.Exp, scale=-1.0))
                    act.activation(u_flat, u_flat, ACT.Ln, bias=1.0).then_inc(cv_l, 1)
                    act.wait_ge(cv_m, 1)
                    act.activation(u_flat, u_flat, ACT.Exp).then_inc(cv_sig, 1)
                if s == 23:
                    act.wait_ge(cv_f, 1)
                    act.copy(oT_hi[:, 4:8, :], u_flat.rearrange("p (f t) -> p f t", f=4)).then_inc(cv_hi, 1)
                if name in ("ogn0", "ogn1"):
                    c = int(name[3])
                    for i in range(2):
                        act.wait_ge(merged, 4 + 2 * c + i + 1)
                        q = 2 * c + i
                        act.copy(hT_hi[:, 2 * q:2 * q + 2, :], Mg[:, 2 * q:2 * q + 2, :]).then_inc(mhi_made, 1)
            for c in range(3):
                act.wait_ge(chunk_used, FFN2 - 4 + c + 1)
                split_hi(FFN2 - 1 + c)
            act.wait_ge(chunk_used, FFN2)
            squares(4, ACC_FLAT, [xn[:, a, :] for a in range(TT)])
            root(5)
            split_hi(FFN2 + 2)
            turned_hi(4, hT_hi, G_FFN)

            def silu_a(n, f, j, it=0):
                t = relu[:, j, :]
                act.wait_ge(chunk_used, (FFN2 + 3 * f + 1 if f else FFN2 + 2) + 6 * it)
                act.activation(t, PS[:, 4 + 2 * j, :], ACT.Abs).then_inc(s_abs, 1)
                act.wait_ge(s_abs, f + 1 + 2 * it)
                act.activation(t, t, ACT.Exp, scale=-1.0).then_inc(s_e, 1)
                act.wait_ge(s_e, f + 1 + 2 * it)
                act.activation(t, t, ACT.Ln, bias=1.0).then_inc(s_ln, 1)

            def silu_b(n, f, j, it=0):
                act.wait_ge(s_min, f + 1 + 2 * it)
                act.activation(relu[:, j, :], relu[:, j, :], ACT.Exp).then_inc(s_sig, 1)
                act.wait_ge(s_prod, f + 1 + 2 * it)
                act.copy(aT_hi[:, j].rearrange("p a t -> p (a t)"), relu[:, j, :]).then_inc(s_hi, 1)

            split_hi(FFN2 + 3)
            silu_a(FFN2, 0, 0)
            split_hi(FFN2 + 4)
            silu_b(FFN2, 0, 0)

            def step2(j, it, f):
                for d in range(2):
                    if FFN2 + 5 + 3 * f + d < FFN2 + 33:
                        if d == 1:
                            silu_a(FFN2, f + 1, (j + 1) % 2, it)
                        split_hi(FFN2 + 5 + 3 * f + d, it)
                    elif d == 1:
                        silu_a(FFN2, f + 1, (j + 1) % 2, it)
                silu_b(FFN2, f + 1, (j + 1) % 2, it)
                if FFN2 + 7 + 3 * f < FFN2 + 33:
                    split_hi(FFN2 + 7 + 3 * f, it)

            with act.Fori(0, 4) as it:
                for j in range(2):
                    step2(j, it, j)
            for f in (8, 9):
                step2(f % 2, 0, f)
            act.wait_ge(chunk_used, FFN2 + 33)
            act.copy(res[:, 0, :], ACC_FLAT[0]).then_inc(out_a, 1)

        @block.vector
        def _(dve):
            links = [0]

            def link(ins):
                links[0] += 1
                ins.then_inc(dve_link, 1)
                dve.wait_ge(dve_link, links[0])

            def split_lo(n, it=0, width=2048):
                width = SHARE if n in POOL_LO else width
                dve.wait_ge(hi_made, n + 1 + 6 * it)
                dve.tensor_tensor(wlo[:, n % RING, 0:width], raw[:, n % RING, 0:width],
                                  whi[:, n % RING, 0:width].bitcast(F32), ALU.subtract).then_inc(lo_made, 1)

            def root(st, squares_sem, squares_n, var_sem, exp_sem, done_sem, count, size):
                dve.wait_ge(squares_sem, squares_n)
                dve.tensor_scalar(st[:, 2:4], st[:, 0:2], 1.0 / size, EPS, ALU.mult, ALU.add).then_inc(var_sem, 1)
                dve.wait_ge(exp_sem, count)
                link(dve.tensor_tensor(st[:, 6:8], st[:, 4:6], st[:, 4:6], ALU.mult))
                link(dve.tensor_tensor(st[:, 6:8], st[:, 6:8], st[:, 2:4], ALU.mult))
                link(dve.tensor_scalar(st[:, 6:8], st[:, 6:8], -0.5, 1.5, ALU.mult, ALU.add))
                dve.tensor_tensor(st[:, 4:6], st[:, 4:6], st[:, 6:8], ALU.mult).then_inc(done_sem, 1)
                dve.wait_ge(done_sem, count)

            def token_root(event):
                root(stat[:, event, :], ssq_made, TT * (event + 1), var_made, exp_made, rs_made, event + 1, D)

            def normed(event, src, dst):
                for a in range(TT):
                    dve.tensor_scalar(dst[a], src[a], stat[:, event, 4 + a:5 + a], None, ALU.mult).then_inc(xn_made, 1)

            def turned_lo(event, hi, lo, gain):
                for q in range(4):
                    dve.wait_ge(trhi_made, 8 * event + 2 * q + 2)
                    for f in range(2):
                        i = dve.scalar_tensor_tensor(
                            lo[:, 2 * q + f, :], PS[:, 6 + q % 2, f * T:(f + 1) * T],
                            prm[:, gain + 2 * q + f:gain + 2 * q + f + 1], hi[:, 2 * q + f, :].bitcast(F32),
                            ALU.mult, ALU.subtract)
                    i.then_inc(trlo_made, 1)

            def evac(name):
                if name in SIG:
                    t, src = relu[:, unit_of[name] % 2, :], lin(unit_of[name])
                    dve.wait_ge(sg_ln, SIG.index(name) + 1)
                    dve.scalar_tensor_tensor(t, src, 0.0, t, ALU.min, ALU.subtract).then_inc(sg_min, 1)

            def evac_end(name):
                if name[:4] == "gout":
                    c, u = int(name[4]), unit_of[name]
                    dve.wait_ge(sg_exp, SIG_EXP.index(name) + 1)
                    dve.tensor_tensor(gsil[:, :, c * CW:(c + 1) * CW], lin(u).rearrange("p (f t) -> p f t", f=2),
                                      relu[:, u % 2, :].rearrange("p (f t) -> p f t", f=2),
                                      ALU.mult).then_inc(drained[u % 2], 1)

            def sb_softplus(h):
                dve.wait_ge(sb_l, h + 1)
                if h >= 2:
                    dve.wait_ge(sb_rc, h - 1)
                dve.scalar_tensor_tensor(sbt[:, h % 2, 1, :], PS[:, h % 2, 0:384], 0.0, sbt[:, h % 2, 0, :],
                                         ALU.max, ALU.add).then_inc(sb_sp, 1)

            def sb_out(j):
                dve.wait_ge(sb_hi, j + 1)
                dve.tensor_tensor(oT_lo[:, j, :], PS[:, 2, 0:256], oT_hi[:, j, :].bitcast(F32),
                                  ALU.subtract).then_inc(sb_lo, 1)

            def gla_gate(a):
                dve.wait_ge(ga_l, a + 1)
                dve.scalar_tensor_tensor(a_ls[:, a, :], PS[:, 6 + a, :], 0.0, relu[:, a, :], ALU.min,
                                         ALU.subtract).then_inc(ga_made, 1)

            def gla_mask(u):
                h, a = u // 2, u % 2
                dve.wait_ge(gs_made, u + 1)
                dve.tensor_tensor(E.rearrange("p l t -> p (l t)"), PS[:, 6:8, :].rearrange("p b n -> p (b n)"),
                                  mask.rearrange("p l t -> p (l t)"), ALU.mult).then_inc(gs_masked, 1)
                if h >= 1:
                    dve.wait_ge(go_made, h)
                if a == 1:
                    dve.tensor_copy(S_gla[:, 2, :], PS[:, 3, 0:128]).then_inc(gs_x, 1)
                dve.wait_ge(gs_masked, u + 1)
                dve.tensor_reduce(S_gla[:, a, :], E.rearrange("p l t -> p t l"), AX, ALU.add).then_inc(gs_ready, 1)

            def gla_norm(h):
                root(gstat[:, h, :], go_ssq, TT * (h + 1), go_var, go_exp, go_rs, h + 1, GLA_DV)
                c = f"gout{h}"
                dve.wait_ge(drained[unit_of[c] % 2], unit_of[c] // 2 + 1)
                for a in range(TT):
                    g = gsil[:, a, h * GLA_DV:(h + 1) * GLA_DV]
                    i = dve.scalar_tensor_tensor(g, PS[:, 3, a * 256:(a + 1) * 256], gstat[:, h, 4 + a:5 + a], g,
                                                 ALU.mult, ALU.mult)
                i.then_inc(go_norm, 1)

            def gla_out(h):
                dve.wait_ge(go_hi, 2 * h + 2)
                for f in range(2):
                    i = dve.scalar_tensor_tensor(
                        oT_lo[:, 4 + 2 * h + f, :], PS[:, 3, f * T:(f + 1) * T], prm[:, G_GLA + f:G_GLA + f + 1],
                        oT_hi[:, 4 + 2 * h + f, :].bitcast(F32), ALU.mult, ALU.subtract)
                i.then_inc(go_lo, 1)

            token_root(0)
            normed(0, [res[:, a, :] for a in range(TT)], [xn[:, a, :] for a in range(TT)])
            split_lo(0, width=1024)
            split_lo(1)
            dve.wait_ge(prm_made, 1)
            dve.tensor_scalar(mhalf[:, :], prm[:, G_MQK:G_MQK + 6], -0.5, None, ALU.mult).then_inc(mhalf_made, 1)
            turned_lo(0, hT_hi, hT_lo, G_MIX)
            split_lo(2)
            for n in range(at["projs0"]):
                evac(list(at)[n])
                split_lo(n + RING)
                evac_end(list(at)[n])
                if n == 1:
                    gla_gate(0)
                    gla_gate(1)
                if 0 <= n - 9 < SB_H:
                    sb_softplus(n - 9)
                if 0 <= n - 12 < SB_H and n % 2 == 0:
                    sb_out((n - 12) // 2)
                if 0 <= n - 10 < 16 and (n - 10) % 2 == 0:
                    gla_mask((n - 10) // 2)
                if 0 <= n - 15 < 12 and (n - 15) % 4 == 0:
                    gla_out((n - 15) // 4)
                if 0 <= n - 13 < 16 and (n - 13) % 4 == 0:
                    gla_norm((n - 13) // 4)
            p0 = at["projs0"]

            def sb_mix(c):
                u = unit_of[f"projs{c}"]
                dve.wait_ge(chunk_used, at[f"projs{c}"] + 1)
                for i in range(2):
                    g = gate_s[:, 4 * c + 2 * i:4 * c + 2 * i + 2, :]
                    dve.tensor_tensor(g, lin(u + i).rearrange("p (f t) -> p f t", f=2), g,
                                      ALU.mult).then_inc(drained[(u + i) % 2], 1)

            sb_mix(0)
            split_lo(p0 + 3)
            gla_out(3)
            sb_mix(1)
            split_lo(p0 + 4)
            for c in range(4):
                u = unit_of[f"projg{c}"]
                gs, gg = gate_s[:, 2 * c:2 * c + 2, :], gate_g[:, 2 * c:2 * c + 2, :]
                dve.wait_ge(chunk_used, at[f"projg{c}"] + 1)
                dve.tensor_tensor(gg, lin(u).rearrange("p (f t) -> p f t", f=2), gg, ALU.mult) \
                   .then_inc(drained[u % 2], 1)
                dve.wait_ge(drained[u % 2], u // 2 + 1)
                dve.tensor_tensor(gs, gs, gg, ALU.add).then_inc(mix_b, 1)
                split_lo(p0 + 5 + c)
                dve.wait_ge(mix_hi, c + 1)
                dve.tensor_tensor(hT_lo[:, 2 * c:2 * c + 2, :], gs, hT_hi[:, 2 * c:2 * c + 2, :].bitcast(F32),
                                  ALU.subtract).then_inc(mix_lo, 1)
                if c == 0:
                    token_root(1)
                    normed(1, [memx[:, a, :] for a in range(TT)], [memx[:, a, :] for a in range(TT)])
            for c in range(3):
                split_lo(p0 + 9 + c)
                if c == 0:
                    turned_lo(1, oT_hi, oT_lo, G_MEM)
            token_root(2)
            normed(2, ACC_FLAT, [xn[:, a, :] for a in range(TT)])
            split_lo(FFN1)
            split_lo(FFN1 + 1)
            split_lo(FFN1 + 2)
            turned_lo(2, hT_hi, hT_lo, G_MLP)

            def square_lo(f, j, it=0):
                dve.wait_ge(h1_relu, f + 1 + 3 * it)
                dve.tensor_tensor(sq[:, j, :], relu[:, j, :], relu[:, j, :], ALU.mult).then_inc(h1_sq, 1)
                dve.wait_ge(h1_sq, f + 1 + 3 * it)
                dve.wait_ge(h1_hi, f + 1 + 3 * it)
                dve.tensor_tensor(aT_lo[:, j].rearrange("p a t -> p (a t)"), sq[:, j, :],
                                  aT_hi[:, j].rearrange("p a t -> p (a t)").bitcast(F32),
                                  ALU.subtract).then_inc(h1_lo, 1)

            square_lo(0, 0)
            split_lo(FFN1 + 3)
            with dve.Fori(0, (F1 - 1) // 3) as it:
                for j in range(3):
                    square_lo(j + 1, (j + 1) % 3, it)
                    split_lo(FFN1 + 4 + 2 * j, it)
                    split_lo(FFN1 + 5 + 2 * j, it)
            token_root(3)
            dve.wait_ge(gfin_in, 16)
            for a in range(TT):
                dve.scalar_tensor_tensor(res[:, a, :], ACC_FLAT[a], stat[:, 3, 4 + a:5 + a], gfin, ALU.mult,
                                         ALU.mult).then_inc(x3_made, 1)
            split_lo(after_ffn1 + 2)
            root(stat[:, 5, :], ssq_made, TT * 5, var_made, exp_made, rs_made, 5, D)
            for a in range(TT):
                dve.tensor_scalar(xn[:, a, :], res[:, a, :], stat[:, 5, 4 + a:5 + a], None, ALU.mult).then_inc(xn_made, 1)

            def evac2_end(name):
                if name[:2] == "cg":
                    u, c = unit_of[name], int(name[2])
                    dve.wait_ge(sg_exp, SIG_EXP.index(name) + 1)
                    v = u_conv[:, 2 * c:2 * c + 2, PAD:PAD + T]
                    dve.tensor_tensor(v, v, relu[:, u % 2, :].rearrange("p (f t) -> p f t", f=2), ALU.mult) \
                       .then_inc(drained[u % 2], 1)
                elif name[0] == "o":
                    u, c = unit_of[name], int(name[3])
                    dve.wait_ge(chunk_used, at[name] + 1)
                    for i in range(2):
                        f = slice(4 * c + 2 * i, 4 * c + 2 * i + 2)
                        d = drained[(u + i) % 2]
                        two = lin(u + i).rearrange("p (f t) -> p f t", f=2)
                        if name[2] == "m":
                            dve.tensor_tensor(Mg[:, f, :], two, Mg[:, f, :], ALU.mult).then_inc(d, 1)
                            continue
                        dve.tensor_tensor(G[:, f, :], two, G[:, f, :], ALU.mult).then_inc(d, 1)
                        dve.wait_ge(d, (u + i) // 2 + 1)
                        dve.tensor_tensor(Mg[:, f, :], Mg[:, f, :], G[:, f, :], ALU.add).then_inc(merged, 1)

            def head_var(e):
                width, size = FN[e][1:3]
                v = scratch(e)[1]
                dve.wait_ge(fn_ln, e + 1)
                dve.tensor_scalar(v, PS[:, 7, 0:width], -1.0 / size, EPS, ALU.mult, ALU.add).then_inc(fn_var, 1)

            def head_norm(e):
                src, width, size, gain = FN[e]
                gain -= G_MQK
                w, v, y = scratch(e)
                dve.wait_ge(fn_var, e + 1)
                dve.wait_ge(fn_exp, e + 1)
                link(dve.tensor_tensor(w, y, y, ALU.mult))
                link(dve.tensor_tensor(w, w, v, ALU.mult))
                link(dve.scalar_tensor_tensor(y, w, -3.0, y, ALU.add, ALU.mult))
                if e in (4, 5):
                    k = kdup["sw"[e - 4]]
                    for g in range(2):
                        r = slice(64 * g, 64 * g + 64)
                        ins = dve.scalar_tensor_tensor(k[r, g, :], k[r, 0, :], mhalf[r, gain:gain + 1], y[r, :],
                                                       ALU.mult, ALU.mult)
                    ins.then_inc(fn_made, 1)
                    return
                if width == 512:
                    y = y.rearrange("p (f t) -> p f t", f=2)
                dve.scalar_tensor_tensor(src, src, mhalf[:, gain:gain + 1], y, ALU.mult, ALU.mult).then_inc(fn_made, 1)

            def att_max_(i):
                kind, a, g = ATT[i]
                dve.wait_ge(att_s, i + 1)
                L = {"m": T, "c": 15}.get(kind, P * (a + 1))
                if kind == "m":
                    src = PS[:, 0:2, :].rearrange("p b (h n) -> p (b h) n", n=T)
                else:
                    if i == 2:
                        dve.wait_ge(mask2_made, 3)
                    dve.wait_ge(att_t, i - 1)
                    src = pbuf[:, i % 2, 0:4 * L].rearrange("p (h n) -> p h n", h=4)
                    m = cmask[:, a, :] if kind == "c" else causal[:, T - L:T]
                    sc = PS[:, 0:2, 0:2 * L].rearrange("p e (h n) -> p e h n", h=2)
                    link(dve.tensor_tensor(src.rearrange("p (h e) n -> p e h n", e=2), sc,
                                           m.unsqueeze(1).unsqueeze(1).to_broadcast([P, 2, 2, L]), ALU.add))
                link(dve.tensor_reduce(amax[:, i, :], src, AX, ALU.max))
                scale = (P if kind == "m" else 64) ** -0.5
                dve.tensor_scalar(amax[:, i, :], amax[:, i, :], -1e29, -scale, ALU.max, ALU.mult).then_inc(att_max, 1)

            def att_scale(i):
                kind, a, g = ATT[i]
                L = {"m": T, "c": 15}.get(kind, P * (a + 1))
                dve.wait_ge(att_e, 4 * i + 4)
                if kind == "c":
                    link(dve.tensor_scalar(aden[:, i, :], aden[:, i, :], 1e-30, None, ALU.max))
                if kind == "m":
                    link(dve.reciprocal(acoef[:, i, :], aden[:, i, :]))
                else:
                    link(dve.reciprocal(aden[:, i, :], aden[:, i, :]))
                    br = "csw".index(kind)
                    gate = gn24[:, 24 * a + 12 * g + br:24 * a + 12 * g + br + 10:3]
                    link(dve.tensor_tensor(acoef[:, i, :], aden[:, i, :], gate, ALU.mult))
                for h in range(4):
                    p = pbuf[:, i % 2, h * L:(h + 1) * L]
                    dve.tensor_scalar(p, p, acoef[:, i, h:h + 1], None, ALU.mult).then_inc(att_p, 1)

            def att_out(i):
                kind, a, g = ATT[i]
                tok = slice(a * P, (a + 1) * P)
                dve.wait_ge(att_hi, group_of(i) + 1)
                if kind == "m":
                    dve.tensor_tensor(oT_lo[:, 8:12, tok], PS[:, 6, :].rearrange("p (h t) -> p h t", h=4),
                                      oT_hi[:, 8:12, tok].bitcast(F32), ALU.subtract).then_inc(att_lo, 1)
                    return
                src = PS[0:64, 6, :].rearrange("p (h e t) -> p e h t", h=2, e=2)
                for e in range(2):
                    r = slice(64 * e, 64 * e + 64)
                    ins = dve.tensor_tensor(oT_lo[r, 2 * g:2 * g + 2, tok], src[:, e],
                                            oT_hi[r, 2 * g:2 * g + 2, tok].bitcast(F32), ALU.subtract)
                ins.then_inc(att_lo, 1)

            def conv_taps(first, last):
                for i in range(first, min(last, 62)):
                    f, k = i % 2, i // 2
                    src = u_conv[:, f, k:k + T]
                    if i == 0:
                        dve.wait_ge(cw_made, 1)
                        dve.wait_ge(drained[unit_of["cg0"] % 2], unit_of["cg0"] // 2 + 1)
                    if k == 0:
                        ins = dve.tensor_scalar(cacc[:, f, :], src, cw[:, f, 0:1], prm[:, B_CONV + f:B_CONV + f + 1],
                                                ALU.mult, ALU.add)
                    else:
                        dve.wait_ge(taps, i - 1)
                        ins = dve.scalar_tensor_tensor(cacc[:, f, :], src, cw[:, f, k:k + 1], cacc[:, f, :],
                                                       ALU.mult, ALU.add)
                    ins.then_inc(taps, 1)

            for n in range(at["vm0"], FFN2 - 4):
                name, s = list(at)[n - 2 * F1], n - at["ca0"]
                evac(name)
                if name[0] == "o":
                    evac2_end(name)
                if s in FN_AT:
                    head_var(FN_AT.index(s))
                if s - 9 in (1, 2):
                    att_scale(s - 10)
                if s - 9 in (0, 1):
                    att_max_(s - 9)
                if 0 <= s - 16 < 12:
                    att_scale(s - 14)
                if 0 <= s - 15 < 12:
                    att_max_(s - 13)
                if s >= 2:
                    conv_taps(4 * (s - 2), 4 * (s - 1))
                split_lo(n + RING)
                if name[0] != "o":
                    evac2_end(name)
                if name == "vm1":
                    turned_lo(3, hT_hi, hT_lo, G_MIX2)
                if s == 0:
                    dve.wait_ge(gn_sum, 1)
                    dve.tensor_scalar(gn24, PS[:, 7, 0:48], -85.0, None, ALU.max).then_inc(gn_clip, 1)
                    dve.wait_ge(gn_exp, 1)
                    link(dve.tensor_scalar(gn24, gn24, 1.0, None, ALU.add))
                    dve.reciprocal(gn24, gn24).then_inc(gn_made, 1)
                if s in FN_AT:
                    head_norm(FN_AT.index(s))
                if name == "qm0":
                    u = unit_of["kcvc"]
                    dve.wait_ge(z_made, 7)
                    dve.wait_ge(drained[u % 2], u // 2 + 1)
                    for b in range(2):
                        for g in range(2):
                            v = Z[b][:, g, :].rearrange("p (i r e) -> p r i e", r=8, e=2)
                            for half in range(2):
                                pos = prm[:, POS + 16 * b + 8 * half:POS + 16 * b + 8 * half + 8]
                                dve.tensor_tensor(blk[b][:, 8 * half:8 * half + 8, 15 * g:15 * g + 15],
                                                  v[:, :, half:half + 15, 0],
                                                  pos.unsqueeze(2).to_broadcast([P, 8, 15]), ALU.add).then_inc(blk_made, 1)
                    for b in range(2):
                        dve.wait_ge(blk_hid, b + 1)
                        dve.tensor_tensor(blk_lo[b], blk[b], blk_hi[b].bitcast(F32), ALU.subtract).then_inc(blk_lod, 1)
                if name in ("wk1", "wv1"):
                    b, u = int(name[1] == "v"), unit_of[name]
                    dve.wait_ge(drained[u % 2], u // 2 + 1)
                    link(dve.tensor_tensor(hwork, hid[b], hid[b], ALU.mult))
                    link(dve.tensor_scalar(hwork, hwork, 0.044715, 1.0, ALU.mult, ALU.add))
                    link(dve.tensor_tensor(hwork, hwork, hid[b], ALU.mult))
                    dve.tensor_scalar(hwork, hwork, -50.0, None, ALU.max).then_inc(h_arg, 1)
                    dve.wait_ge(h_exp, b + 1)
                    link(dve.tensor_scalar(hwork, hwork, 1.0, None, ALU.add))
                    link(dve.reciprocal(hwork, hwork))
                    dve.tensor_tensor(hid[b], hid[b], hwork, ALU.mult).then_inc(h_made, 1)
                    dve.wait_ge(h_made, b + 1)
                if s - 9 in (3, 4):
                    att_out(s - 12)
                if 0 <= s - 18 < 12 and ATT[s - 16][0] == "c":
                    att_out(s - 16)
                if s == 20:
                    dve.wait_ge(cv_mean, 1)
                    m = PS[:, 7, 0:T].unsqueeze(1).to_broadcast([P, 4, T])
                    dve.wait_ge(taps_b, 92)
                    dve.scalar_tensor_tensor(cacc, m, 1.0 / 512, cacc, ALU.mult, ALU.add).then_inc(cv_mid, 1)
                if s == 21:
                    dve.wait_ge(cv_mean, 2)
                    v, y, w = (u_flat[:, T * i:T * i + T] for i in range(3))
                    dve.tensor_scalar(v, PS[:, 7, 0:T], -1.0 / 512, 1e-5, ALU.mult, ALU.add).then_inc(cv_var, 1)
                    dve.wait_ge(cv_exp, 1)
                    link(dve.tensor_tensor(w, y, y, ALU.mult))
                    link(dve.tensor_tensor(w, w, v, ALU.mult))
                    link(dve.tensor_scalar(w, w, -0.5, 1.5, ALU.mult, ALU.add))
                    link(dve.tensor_tensor(y, y, w, ALU.mult))
                    dve.tensor_tensor(cacc, cacc, y.unsqueeze(1).to_broadcast([P, 4, T]), ALU.mult).then_inc(cv_y, 1)
                if s == 22:
                    dve.wait_ge(cv_l, 1)
                    dve.scalar_tensor_tensor(u_flat, cacc_flat, 0.0, u_flat, ALU.min, ALU.subtract).then_inc(cv_m, 1)
                    dve.wait_ge(cv_sig, 1)
                    dve.tensor_tensor(u_flat, u_flat, cacc_flat, ALU.mult).then_inc(cv_f, 1)
                if s == 23:
                    dve.wait_ge(cv_hi, 1)
                    dve.tensor_tensor(oT_lo[:, 4:8, :], u_flat.rearrange("p (f t) -> p f t", f=4),
                                      oT_hi[:, 4:8, :].bitcast(F32), ALU.subtract).then_inc(cv_lo, 1)
                if name in ("ogn0", "ogn1"):
                    c = int(name[3])
                    for i in range(2):
                        q = 2 * c + i
                        dve.wait_ge(mhi_made, q + 1)
                        dve.tensor_tensor(hT_lo[:, 2 * q:2 * q + 2, :], Mg[:, 2 * q:2 * q + 2, :],
                                          hT_hi[:, 2 * q:2 * q + 2, :].bitcast(F32), ALU.subtract).then_inc(mlo_made, 1)
            for c in range(3):
                split_lo(FFN2 - 1 + c)
            root(stat[:, 4, :], ssq_made, TT * 6, var_made, exp_made, rs_made, 6, D)
            normed(4, ACC_FLAT, [xn[:, a, :] for a in range(TT)])
            split_lo(FFN2 + 2)
            turned_lo(4, hT_hi, hT_lo, G_FFN)

            def silu_a(f, j, it=0):
                t = relu[:, j, :]
                dve.wait_ge(s_ln, f + 1 + 2 * it)
                dve.scalar_tensor_tensor(t, PS[:, 4 + 2 * j, :], 0.0, t, ALU.min, ALU.subtract).then_inc(s_min, 1)

            def silu_b(f, j, it=0):
                t = relu[:, j, :]
                dve.wait_ge(s_sig, f + 1 + 2 * it)
                dve.tensor_tensor(t, PS[:, 4 + 2 * j, :], t, ALU.mult).then_inc(s_mul, 1)
                dve.wait_ge(s_mul, f + 1 + 2 * it)
                dve.tensor_tensor(t, PS[:, 5 + 2 * j, :], t, ALU.mult).then_inc(s_prod, 1)
                dve.wait_ge(s_hi, f + 1 + 2 * it)
                dve.tensor_tensor(aT_lo[:, j].rearrange("p a t -> p (a t)"), t,
                                  aT_hi[:, j].rearrange("p a t -> p (a t)").bitcast(F32),
                                  ALU.subtract).then_inc(s_lo, 1)

            split_lo(FFN2 + 3)
            silu_a(0, 0)
            split_lo(FFN2 + 4)
            silu_b(0, 0)

            def step2(j, it, f):
                m = FFN2 + 5 + 3 * f
                if m < FFN2 + 33:
                    split_lo(m, it)
                silu_a(f + 1, (j + 1) % 2, it)
                if m + 1 < FFN2 + 33:
                    split_lo(m + 1, it)
                silu_b(f + 1, (j + 1) % 2, it)
                if m + 2 < FFN2 + 33:
                    split_lo(m + 2, it)

            with dve.Fori(0, 4) as it:
                for j in range(2):
                    step2(j, it, j)
            for f in (8, 9):
                step2(f % 2, 0, f)
            dve.wait_ge(chunk_used, FFN2 + 33)
            dve.tensor_copy(res[:, 1, :], ACC_FLAT[1]).then_inc(out_b, 1)
    return nc


_INS = ["x", "norm_mix", "w_in", "w_gate_up", "b_gate_up", "gla_norm", "w_proj_sb", "w_proj_gla", "w_out",
        "norm_mlp", "w_ff1", "w_ff2", "norm_final", "mem_2", "norm_mix_2", "w_in_2", "nsa_qk_norm_2", "cmp_pos_2",
        "cmp_w1_2", "cmp_w2_2", "w_nsa_out_2", "conv_w_2", "conv_b_2", "conv_ln_g_2", "conv_ln_b_2",
        "w_conv_out_2", "norm_mem_2", "w_mem_kv_2", "mem_qk_norm_2", "w_mem_out_2", "w_out_2", "norm_ffn_2",
        "w_gate_2", "w_up_2", "w_down_2"]
_OUTS = [((1, 256, 1024), "float32")]


def kernel(**inputs):
    import numpy as _np
    import concourse.bacc as _bacc
    from concourse import mybir as _mybir
    from concourse.bass_utils import run_bass_kernel_spmd as _run

    nc = _bacc.Bacc("TRN2", target_bir_lowering=False, num_devices=1)
    arrays, args = {}, []
    for name in _INS:
        a = _np.ascontiguousarray(inputs[name])
        arrays[f"in_{name}_dram"] = a
        args.append(nc.dram_tensor(f"in_{name}_dram", a.shape, _mybir.dt.from_np(a.dtype), kind="ExternalInput").ap())
    for i, (shape, dtype) in enumerate(_OUTS):
        dt = _mybir.dt.from_np(_np.dtype(dtype))
        args.append(nc.dram_tensor(f"out_{i}_dram", shape, dt, kind="ExternalOutput").ap())
    two_block_kernel(nc, *args)
    r = _run(nc, [arrays], core_ids=[0])
    got = tuple(r.results[0][f"out_{i}_dram"] for i in range(len(_OUTS)))
    return got[0]
```
